# Optimizing a Trainium2 kernel written in Bass

```python
import math
import jax, jax.numpy as jnp
from jax import lax
import numpy as np

D_MODEL = 2048
BATCH = 1
SEQ = 512
DEPTH = 1
DEC_BATCH = 8
DEC_SEQ = 4
PAST_LEN = 4096
PAGE_SIZE = 128

MIX_WIDTH = D_MODEL
GROUP_WIDTH = MIX_WIDTH // 4
HEAD_DIM = 128
N_HEADS_GRP = GROUP_WIDTH // HEAD_DIM
CHUNK_A = 128
POOL_WINDOWS = (2, 4, 8, 16)
POOL_STATE = max(POOL_WINDOWS) - 1
MLSTM_CHUNK = 64
CONV_W = 3
D_FF = ((8 * D_MODEL // 3) + 127) // 128 * 128
N_MEM = 256
MEM_HEADS = 4
MEM_HEAD_DIM = 128
MEM_WIDTH = MEM_HEADS * MEM_HEAD_DIM
N_IN = 10 * GROUP_WIDTH + 2 * N_HEADS_GRP
EPS = 1e-6

kernel_name = 'hybrid_headgroup_decoder_step'

def rms_norm(x, g):
    xf = x.astype(jnp.float32)
    y = xf * lax.rsqrt(jnp.mean(xf * xf, axis=-1, keepdims=True) + EPS)
    return (y * g.astype(jnp.float32)).astype(x.dtype)

def chunk_spatial_gate(u, v, w_s, b_s):
    n, t, h, d = v.shape
    t_pad = -(-t // CHUNK_A) * CHUNK_A
    vp = jnp.pad(v, ((0, 0), (0, t_pad - t), (0, 0), (0, 0)))
    vc = vp.reshape(n, t_pad // CHUNK_A, CHUNK_A, h, d)
    mask = jnp.tril(jnp.ones((CHUNK_A, CHUNK_A), dtype=bool))
    w = jnp.where(mask, w_s, 0).astype(v.dtype)
    mixed = jnp.einsum('hts,ncshd->ncthd', w, vc) + b_s.T[None, None, :, :, None].astype(v.dtype)
    mixed = mixed.reshape(n, t_pad, h, d)[:, :t]
    return u * mixed

def multiscale_pool(x, prefix, n_valid):
    n, t, c = x.shape
    p = prefix.shape[1]
    g_w = c // len(POOL_WINDOWS)
    xx = jnp.concatenate([prefix.astype(x.dtype), x], axis=1)
    xf = xx.astype(jnp.float32).reshape(n, p + t, len(POOL_WINDOWS), g_w)
    cs = jnp.concatenate([jnp.zeros_like(xf[:, :1]), jnp.cumsum(xf, axis=1)], axis=1)
    run_end = cs[:, p + 1:p + 1 + t]
    avail = jnp.arange(t, dtype=jnp.float32)[None, :, None] + (1.0 + n_valid)
    outs = []
    for g, w in enumerate(POOL_WINDOWS):
        run_start = cs[:, p + 1 - w:p + 1 - w + t, g]
        outs.append((run_end[:, :, g] - run_start) / jnp.minimum(avail, float(w)))
    mean = jnp.stack(outs, axis=2).reshape(n, t, c)
    return (mean - x.astype(jnp.float32)).astype(x.dtype), xx[:, -POOL_STATE:]

def causal_dwconv(x, prefix, w):
    k = w.shape[0]
    t = x.shape[1]
    xx = jnp.concatenate([prefix.astype(x.dtype), x], axis=1)
    y = xx[:, 0:t] * w[0]
    for j in range(1, k):
        y = y + xx[:, j:j + t] * w[j]
    return y, xx[:, -(k - 1):]

def mlstm_chunkwise(q, k, v, i_pre, log_f, c0, n0, m0):
    nb, t, h, d = q.shape
    L = math.gcd(t, MLSTM_CHUNK)
    nc = t // L

    def to_chunks(a):
        return jnp.moveaxis(a.reshape((nb, nc, L) + a.shape[2:]), 1, 0)

    xs = (to_chunks(q), to_chunks(k), to_chunks(v), to_chunks(i_pre), to_chunks(log_f))
    causal = jnp.tril(jnp.ones((L, L), dtype=bool))

    def step(carry, inp):
        c, nv, m = carry
        qc, kc, vc, ic, fc = inp
        b = jnp.cumsum(fc, axis=1)
        log_d = b[:, :, None, :] - b[:, None, :, :] + ic[:, None, :, :]
        log_d = jnp.where(causal[None, :, :, None], log_d, -jnp.inf)
        log_inter = b + m[:, None, :]
        m_t = jnp.maximum(log_inter, jnp.max(log_d, axis=2))
        dmat = jnp.exp(log_d - m_t[:, :, None, :])
        inter = jnp.exp(log_inter - m_t)
        s = jnp.einsum('nthd,nshd->ntsh', qc, kc) * dmat
        num = jnp.einsum('ntsh,nshd->nthd', s, vc) + inter[..., None] * jnp.einsum('nthd,nhed->nthe', qc, c)
        den = jnp.sum(s, axis=2) + inter * jnp.einsum('nthd,nhd->nth', qc, nv)
        hout = num / jnp.maximum(jnp.abs(den), jnp.exp(-m_t))[..., None]
        m_new = m_t[:, -1]
        decay = jnp.exp(b[:, -1] + m - m_new)
        wts = jnp.exp(b[:, -1:, :] - b + ic - m_new[:, None, :])
        c_new = decay[..., None, None] * c + jnp.einsum('nsh,nshe,nshd->nhed', wts, vc, kc)
        n_new = decay[..., None] * nv + jnp.einsum('nsh,nshd->nhd', wts, kc)
        return (c_new, n_new, m_new), hout

    (c, nv, m), hs = lax.scan(step, (c0, n0, m0), xs)
    hs = jnp.moveaxis(hs, 0, 1).reshape(nb, t, h, d)
    return hs, c, nv, m

def mix_block(hn, w_in, w_s, b_s, w_pool, pool_scale, b_gate, mlstm_norm, w_dconv, w_out,
              pool_prefix, pool_valid, conv_prefix, c0, n0, m0):
    f32 = jnp.float32
    nb, t, _ = hn.shape
    gw = GROUP_WIDTH
    z = hn @ w_in
    a_u, a_v, b_x, c_q, c_k, c_v, c_o, d_b, d_c, d_x = [z[..., j * gw:(j + 1) * gw] for j in range(10)]
    gates = (z[..., 10 * gw:] + b_gate).astype(f32)
    i_pre, f_pre = gates[..., :N_HEADS_GRP], gates[..., N_HEADS_GRP:]

    def heads(a):
        return a.reshape(nb, t, N_HEADS_GRP, HEAD_DIM)

    v_rows = jax.nn.gelu(a_v)
    y_a = chunk_spatial_gate(heads(jax.nn.gelu(a_u)), heads(v_rows), w_s, b_s).reshape(nb, t, gw)
    pooled, pool_state = multiscale_pool(b_x, pool_prefix, pool_valid)
    y_b = jnp.einsum('ntgc,gce->ntge', heads(pooled), w_pool).reshape(nb, t, gw) * pool_scale
    q = heads(c_q).astype(f32)
    k = heads(c_k).astype(f32) * HEAD_DIM ** -0.5
    v = heads(c_v).astype(f32)
    h_c, c1, n1, m1 = mlstm_chunkwise(q, k, v, i_pre, jax.nn.log_sigmoid(f_pre), c0, n0, m0)
    h_c = h_c * lax.rsqrt(jnp.mean(h_c * h_c, axis=-1, keepdims=True) + EPS)
    y_c = (jax.nn.sigmoid(c_o.astype(f32)) * h_c.reshape(nb, t, gw) * mlstm_norm.astype(f32)).astype(hn.dtype)
    conv_out, conv_state = causal_dwconv(d_c * d_x, conv_prefix, w_dconv)
    y_d = d_b * conv_out
    out = jnp.concatenate([y_a, y_b, y_c, y_d], axis=-1) @ w_out
    return out, v_rows, pool_state, conv_state, c1, n1, m1

def mem_kv(mem, g, w_kv):
    nb, m, _ = mem.shape
    kv = rms_norm(mem, g) @ w_kv
    k, v = jnp.split(kv, 2, axis=-1)
    return k.reshape(nb, m, MEM_HEADS, MEM_HEAD_DIM), v.reshape(nb, m, MEM_HEADS, MEM_HEAD_DIM)

def cross_attend(hn, k, v, w_q, w_o):
    nb, t, _ = hn.shape
    q = (hn @ w_q).reshape(nb, t, MEM_HEADS, MEM_HEAD_DIM)
    s = jnp.einsum('nthd,nmhd->nhtm', q, k.astype(q.dtype), preferred_element_type=jnp.float32) * MEM_HEAD_DIM ** -0.5
    p = jax.nn.softmax(s, axis=-1).astype(hn.dtype)
    o = jnp.einsum('nhtm,nmhd->nthd', p, v.astype(hn.dtype))
    return o.reshape(nb, t, MEM_WIDTH) @ w_o

def conv_ffn(hn, w_up, w_fconv, w_down, prefix):
    up = hn @ w_up
    up_c, state = causal_dwconv(up, prefix, w_fconv)
    g, u = jnp.split(up_c, 2, axis=-1)
    return (jax.nn.silu(g) * u) @ w_down, state

def decoder_layer(x, mk, mv, pool_prefix, pool_valid, conv_prefix, c0, n0, m0, ffn_prefix, lw):
    (norm_mix, w_in, w_s, b_s, w_pool, pool_scale, b_gate, mlstm_norm, w_dconv, w_out,
     norm_cross, w_q, w_o, norm_ffn, w_up, w_fconv, w_down) = lw
    mix, v_rows, pool_st, conv_st, c1, n1, m1 = mix_block(
        rms_norm(x, norm_mix), w_in, w_s, b_s, w_pool, pool_scale, b_gate, mlstm_norm, w_dconv, w_out,
        pool_prefix, pool_valid, conv_prefix, c0, n0, m0)
    x = x + mix
    x = x + cross_attend(rms_norm(x, norm_cross), mk, mv, w_q, w_o)
    ffn, ffn_st = conv_ffn(rms_norm(x, norm_ffn), w_up, w_fconv, w_down, ffn_prefix)
    x = x + ffn
    return x, v_rows, pool_st, conv_st, c1, n1, m1, ffn_st

def setup_inputs(seed: int = 0) -> dict:
    key = jax.random.key(seed)
    ks = iter(jax.random.split(key, 40))

    def nrm(shape, scale):
        return scale * jax.random.normal(next(ks), shape, jnp.float32)

    H, Dh, gw = N_HEADS_GRP, HEAD_DIM, GROUP_WIDTH
    return {
        'x_prompt': nrm((BATCH, SEQ, D_MODEL), 1.0),
        'x_sample': nrm((DEC_BATCH, DEC_SEQ, D_MODEL), 1.0),
        'mem_prompt': nrm((BATCH, N_MEM, D_MODEL), 1.0),
        'state_pool': nrm((DEPTH, DEC_BATCH, POOL_STATE, gw), 1.0),
        'state_conv': nrm((DEPTH, DEC_BATCH, CONV_W - 1, gw), 1.0),
        'state_mlstm_c': nrm((DEPTH, DEC_BATCH, H, Dh, Dh), 0.3),
        'state_mlstm_n': nrm((DEPTH, DEC_BATCH, H, Dh), 0.3),
        'state_mlstm_m': nrm((DEPTH, DEC_BATCH, H), 0.5),
        'state_ffn_conv': nrm((DEPTH, DEC_BATCH, CONV_W - 1, 2 * D_FF), 1.0),
        'cache_mem_k': nrm((DEPTH, DEC_BATCH, N_MEM, MEM_HEADS, MEM_HEAD_DIM), 1.0),
        'cache_mem_v': nrm((DEPTH, DEC_BATCH, N_MEM, MEM_HEADS, MEM_HEAD_DIM), 1.0),
        'norm_mix': 1.0 + nrm((DEPTH, D_MODEL), 0.01),
        'w_in': nrm((DEPTH, D_MODEL, N_IN), D_MODEL ** -0.5),
        'w_s': nrm((DEPTH, H, CHUNK_A, CHUNK_A), 0.5 * CHUNK_A ** -0.5),
        'b_s': 1.0 + nrm((DEPTH, H, CHUNK_A), 0.01),
        'w_pool': nrm((DEPTH, H, Dh, Dh), Dh ** -0.5),
        'pool_scale': 0.5 + nrm((DEPTH, gw), 0.01),
        'b_gate': jnp.concatenate([nrm((DEPTH, H), 0.1), 3.0 + nrm((DEPTH, H), 0.1)], axis=-1),
        'mlstm_norm': 1.0 + nrm((DEPTH, gw), 0.01),
        'w_dconv': nrm((DEPTH, CONV_W, gw), CONV_W ** -0.5),
        'w_out': nrm((DEPTH, MIX_WIDTH, D_MODEL), MIX_WIDTH ** -0.5),
        'mem_norm': 1.0 + nrm((DEPTH, D_MODEL), 0.01),
        'w_kv': nrm((DEPTH, D_MODEL, 2 * MEM_WIDTH), D_MODEL ** -0.5),
        'norm_cross': 1.0 + nrm((DEPTH, D_MODEL), 0.01),
        'w_q': nrm((DEPTH, D_MODEL, MEM_WIDTH), D_MODEL ** -0.5),
        'w_o': nrm((DEPTH, MEM_WIDTH, D_MODEL), MEM_WIDTH ** -0.5),
        'norm_ffn': 1.0 + nrm((DEPTH, D_MODEL), 0.01),
        'w_up': nrm((DEPTH, D_MODEL, 2 * D_FF), D_MODEL ** -0.5),
        'w_fconv': nrm((DEPTH, CONV_W, 2 * D_FF), CONV_W ** -0.5),
        'w_down': nrm((DEPTH, D_FF, D_MODEL), D_FF ** -0.5),
        'final_norm': 1.0 + nrm((D_MODEL,), 0.01),
    }

def reference(x_prompt, x_sample, mem_prompt, state_pool, state_conv, state_mlstm_c, state_mlstm_n,
              state_mlstm_m, state_ffn_conv, cache_mem_k, cache_mem_v, norm_mix, w_in, w_s, b_s, w_pool,
              pool_scale, b_gate, mlstm_norm, w_dconv, w_out, mem_norm, w_kv, norm_cross, w_q, w_o,
              norm_ffn, w_up, w_fconv, w_down, final_norm):
    f32 = jnp.float32
    nb = x_prompt.shape[0]
    pdt = x_prompt.dtype
    xp, xs = x_prompt, x_sample
    p_pool, p_conv, p_c, p_n, p_m, p_ffn, p_mk, p_mv = [], [], [], [], [], [], [], []
    s_v, s_pool, s_conv, s_c, s_n, s_m, s_ffn = [], [], [], [], [], [], []
    for l in range(DEPTH):
        lw = (norm_mix[l], w_in[l], w_s[l], b_s[l], w_pool[l], pool_scale[l], b_gate[l], mlstm_norm[l],
              w_dconv[l], w_out[l], norm_cross[l], w_q[l], w_o[l], norm_ffn[l], w_up[l], w_fconv[l], w_down[l])
        mk, mv = mem_kv(mem_prompt, mem_norm[l], w_kv[l])
        xp, _, pool_st, conv_st, c1, n1, m1, ffn_st = decoder_layer(
            xp, mk, mv,
            jnp.zeros((nb, POOL_STATE, GROUP_WIDTH), pdt), 0,
            jnp.zeros((nb, CONV_W - 1, GROUP_WIDTH), pdt),
            jnp.zeros((nb, N_HEADS_GRP, HEAD_DIM, HEAD_DIM), f32),
            jnp.zeros((nb, N_HEADS_GRP, HEAD_DIM), f32),
            jnp.zeros((nb, N_HEADS_GRP), f32),
            jnp.zeros((nb, CONV_W - 1, 2 * D_FF), pdt), lw)
        p_pool.append(pool_st); p_conv.append(conv_st); p_ffn.append(ffn_st)
        p_c.append(c1.astype(pdt)); p_n.append(n1.astype(pdt)); p_m.append(m1.astype(pdt))
        p_mk.append(mk); p_mv.append(mv)
        xs, v_rows, pool_st, conv_st, c1, n1, m1, ffn_st = decoder_layer(
            xs, cache_mem_k[l], cache_mem_v[l],
            state_pool[l], POOL_STATE, state_conv[l],
            state_mlstm_c[l].astype(f32), state_mlstm_n[l].astype(f32), state_mlstm_m[l].astype(f32),
            state_ffn_conv[l], lw)
        s_v.append(v_rows); s_pool.append(pool_st); s_conv.append(conv_st); s_ffn.append(ffn_st)
        s_c.append(c1.astype(state_mlstm_c.dtype)); s_n.append(n1.astype(state_mlstm_n.dtype))
        s_m.append(m1.astype(state_mlstm_m.dtype))
    y_prompt = rms_norm(xp, final_norm)
    y_sample = rms_norm(xs, final_norm)
    return (y_prompt, y_sample,
            jnp.stack(p_pool), jnp.stack(p_conv), jnp.stack(p_c), jnp.stack(p_n), jnp.stack(p_m),
            jnp.stack(p_ffn), jnp.stack(p_mk), jnp.stack(p_mv),
            jnp.stack(s_v), jnp.stack(s_pool), jnp.stack(s_conv), jnp.stack(s_c), jnp.stack(s_n),
            jnp.stack(s_m), jnp.stack(s_ffn))


_drawn_inputs = setup_inputs


def setup_inputs(seed=0):
    import zlib

    import numpy as np

    out = dict(_drawn_inputs(seed))
    spreads = {}
    factors = {'norm_mix': 3.759,
     'b_s': 40.979,
     'pool_scale': 54.257,
     'mlstm_norm': 64.0,
     'mem_norm': 22.402,
     'norm_cross': 31.791,
     'norm_ffn': 128.926,
     'final_norm': 188.846,
     'cache_mem_k': 3.006,
     'cache_mem_v': 3.071}
    for name, (base, spread) in spreads.items():
        noise = np.random.default_rng([zlib.crc32(name.encode()), seed]).standard_normal(out[name].shape)
        drawn = base * np.exp(spread * noise) if base else spread * noise
        out[name] = __import__('jax').numpy.asarray(drawn.astype(out[name].dtype))
    for name, factor in factors.items():
        out[name] = (out[name] * factor).astype(out[name].dtype)
    return out
```

```python
from contextlib import ExitStack

import numpy as np

import concourse.bass as bass
from concourse import mybir

F32 = mybir.dt.float32
F32R = mybir.dt.float32r
ALU = mybir.AluOpType
ACT = mybir.ActivationFunctionType
AX = mybir.AxisListType

P = 128
D = 2048
KD = D // P
SEQ = 512
NB, NT = 8, 4
NS = NB * NT
T = SEQ + NS
TH = T // 2
H = 4
GW = H * P
NM = 256
MT = NM // P
DFF = 5504
JF = DFF // P
CH = SEQ // P
PST = 15
EPS = 1e-6
SCALE = float(P) ** -0.5

UB = 8
RING = 4
GRP = 8
NG = JF // GRP
REST = JF - NG * GRP

U_MEM, O_MEM = 0, 0
U_GATE, O_GATE = U_MEM + 2 * 8, O_MEM + 8
U_PRE, O_PRE = U_GATE + 2, O_GATE + 1
U_MIX, O_MIX = U_PRE + 2 * 2 * H, O_PRE + 2 * H
PAN = 8
U_OUT, O_OUT = U_MIX + 2 * PAN * H, O_MIX + PAN * H
U_Q, O_Q = U_OUT + 2 * KD, O_OUT + KD
U_O, O_O = U_Q + 2 * H, O_Q + H
U_FFN, O_FFN = U_O + KD // 2, O_O + KD
FU, FO = 2 * 2 * GRP + KD, 2 * GRP + KD
U_LAST, O_LAST = U_FFN + NG * FU, O_FFN + NG * FO
U_LDN, O_LDN = U_LAST + 4 * REST, O_LAST + 2 * REST
N_UNITS = U_LDN + KD // 2

C_ID, C_ONE, C_TRI = 0, P, 2 * P
C_STRI = 3 * P
C_BLK = C_STRI + NS
C_PF = C_BLK + NB
C_PW = C_PF + 4 * H
C_INV = C_PW + H
C_EPS = C_INV + (PST + 1) * H
N_CST = C_EPS + 2
V_MEM, V_MIX, V_CROSS, V_FFN, V_FIN = [KD * n for n in range(5)]
V_BG = 5 * KD
V_PS = V_BG + 1
V_MN = V_PS + H
V_DC = V_MN + H
N_VEC = V_DC + 3 * H

EP = PST + SEQ
ES = PST + NT
PEXT = EP + NB * ES
CP = 2 + SEQ
CS = 2 + NT
CEXT = CP + NB * CS
CV = CEXT - 2


class Index:

    def __init__(self, const, reg=None, step=0):
        self.const, self.reg, self.step = const, reg, step

    def __add__(self, k):
        return Index(self.const + k, self.reg, self.step)

    def __sub__(self, k):
        return self + (-k)

    def value(self):
        return self.const if self.reg is None else self.reg * self.step + self.const

    def mod(self, m):
        assert self.step % m == 0
        return self.const % m

    def over(self, m):
        assert self.step % m == 0
        return Index(self.const // m, self.reg, self.step // m)

    def times(self, m):
        return Index(self.const * m, self.reg, self.step * m)


class Chain:

    def __init__(self, eng, sem):
        self.eng, self.sem, self.at = eng, sem, Index(0)

    def __call__(self, ins):
        ins.then_inc(self.sem, 1)
        self.at = self.at + 1
        self.eng.wait_ge(self.sem, self.at.value())

    def enter(self, reg, per, first=0):
        self.start, self.per = self.at.const, per
        self.at = Index(self.at.const - first * per, reg, per)

    def leave(self, times, first=0):
        used = self.at.const - (self.start - first * self.per)
        assert used == self.per, f"links in a round: {used}, not {self.per}"
        self.at = Index(self.start + times * self.per)


class Place:

    def __init__(self, at, spans):
        self.at, self.spans = at, [list(s) for s in spans]

    def take(self, name, shape, dt=F32):
        n = -(-int(np.prod(shape[1:])) * 4 // 32) * 32
        for s in self.spans:
            if s[1] - s[0] >= n:
                s[0] += n
                return self.at(name, s[0] - n, shape, dt)
        raise ValueError(f"no room for {name}")


def build(nc, ins, outs):
    ctx = ExitStack()
    with ctx:
        def sem(name):
            return ctx.enter_context(nc.semaphore(name))

        base = -(-nc.sbuf_base // 64) * 64

        def at(name, offset, shape, dt=F32):
            return nc.alloc_sbuf_tensor_at(name, shape, dt, offset=base + offset)

        ACT_B, UNIT_B = KD * T * 4, UB * P * 4
        R_X = 0
        R_AH = R_X + ACT_B
        R_AL = R_AH + ACT_B
        R_Y = R_AL + ACT_B
        R_RAW = R_Y + ACT_B
        R_WH = R_RAW + RING * UNIT_B
        R_WL = R_WH + RING * UNIT_B
        R_CST = R_WL + RING * UNIT_B
        R_VEC = R_CST + -(-N_CST * 4 // 32) * 32
        R_RSTD = R_VEC + -(-N_VEC * 4 // 32) * 32
        R_SQA = R_RSTD + T * 4
        R_MKV = R_SQA + T * 4
        R_FREE = R_MKV + 2 * H * NM * 4
        R_END = (nc.sbuf_usable_end - base) // 32 * 32
        R_SQT = R_END - 2 * T * 4

        x_t = at("x_t", R_X, [P, KD, T])
        a_hi = at("a_hi", R_AH, [P, KD, T], F32R)
        a_lo = at("a_lo", R_AL, [P, KD, T], F32R)
        m_raw = at("m_raw", R_AL, [P, KD, NM])
        y_t = at("y_t", R_Y, [P, KD, T])
        m_hi = at("m_hi", R_Y, [P, KD, NM], F32R)
        m_lo = at("m_lo", R_Y + KD * NM * 4, [P, KD, NM], F32R)
        kc_t = at("kc_t", R_Y, [P, H, NB, NM])
        h_hi = at("h_hi", R_Y, [P, GRP, T], F32R)
        h_lo = at("h_lo", R_Y + GRP * T * 4, [P, GRP, T], F32R)
        w_raw = at("w_raw", R_RAW, [P, RING, UB * P])
        w_hi = at("w_hi", R_WH, [P, RING, UB * P], F32R)
        w_lo = at("w_lo", R_WL, [P, RING, UB * P], F32R)
        cst = at("cst", R_CST, [P, N_CST])
        vec = at("vec", R_VEC, [P, N_VEC])
        rstd = at("rstd", R_RSTD, [P, T])
        sq_sum = at("sq_sum", R_SQA, [P, T])
        mk_t = at("mk_t", R_MKV, [P, H, NM])
        mv_t = at("mv_t", R_MKV + H * NM * 4, [P, MT, GW])
        sq_tmp = at("sq_tmp", R_SQT, [P, 2, T])
        vt_mem = at("vt_mem", R_FREE, [P, H, NM])
        rstd_m = rstd[:, 0:NM]
        assert R_FREE + H * NM * 4 <= R_SQT

        mix = Place(at, [(R_X, R_AH), (R_FREE, R_END)])
        qkv = mix.take("qkv", [P, 3, T])
        rows = mix.take("rows", [P, 3, T])
        q_in = mix.take("q_in", [P, T])
        k_tok = mix.take("k_tok", [P, CH + 1, P])
        v_tok = mix.take("v_tok", [P, CH + 1, P])
        dmat = mix.take("dmat", [P, CH, P])
        dmat_s = mix.take("dmat_s", [NS, NS])
        state = mix.take("state", [P, CH, P + 1])
        c_smp = mix.take("c_smp", [P, NB, P])
        n_smp = mix.take("n_smp", [P, H, NB])
        cols = mix.take("cols", [P, 2, CH + 1, H])
        nq = mix.take("nq", [P, NS])
        h_tmp = mix.take("h_tmp", [P, NS])
        va_t = mix.take("va_t", [P, T])
        va_tok = mix.take("va_tok", [P, CH + 1, P])
        bs_t = mix.take("bs_t", [P, T])
        ws_t = mix.take("ws_t", [P, P])
        wd_t = mix.take("wd_t", [NS, NS])
        wp_t = mix.take("wp_t", [P, P])
        pe1 = mix.take("pe1", [P, PEXT])
        pe2 = mix.take("pe2", [P, PEXT])
        dx_e, dcv = pe1[:, 0:CEXT], pe2[:, 0:CEXT]
        den_t, h_t = qkv[:, 1, 0:SEQ], qkv[:, 1, :]
        vws = [qkv[:, 2, 0:4 * P], qkv[:, 0, 0:4 * P]]

        gt = Place(at, [(R_X + 3 * T * 4, R_AH)])
        gate = gt.take("gate", [P, T])
        scan_p = [gt.take(f"scan_p{n}", [H, CH, P // 2 + P]) for n in range(2)]
        scan_s = [gt.take(f"scan_s{n}", [H, NB, 2 + NT]) for n in range(2)]
        f_row = gt.take("f_row", [H, T])
        b_row = gt.take("b_row", [H, T])
        a_row = gt.take("a_row", [H, T])
        m_row = gt.take("m_row", [H, T])
        w_row = gt.take("w_row", [H, T])
        r3 = gt.take("r3", [H, 3, T])
        m_prev = gt.take("m_prev", [H, CH])
        ms_in = gt.take("ms_in", [H, NB])

        q_t = at("q_t", R_FREE, [P, H, T])
        assert R_FREE + H * T * 4 <= R_END
        vc_t = at("vc_t", R_AH, [P, NB, MT, GW])
        assert NB * MT * GW * 4 <= ACT_B
        o_hi = at("o_hi", R_AL, [P, H, T], F32R)
        o_lo = at("o_lo", R_AL + H * T * 4, [P, H, T], F32R)
        cross = Place(at, [(R_AL + 2 * H * T * 4, R_Y)])
        prob = cross.take("prob", [P, H, NM])
        prob_t = cross.take("prob_t", [P, H * MT, P])
        q_pad = cross.take("q_pad", [P, H, NB, NS])
        top = cross.take("top", [P, H])
        neg_top = cross.take("neg_top", [P, H])
        p_sum = cross.take("p_sum", [P, H])
        p_inv = cross.take("p_inv", [P, H])

        ffn = Place(at, [(R_MKV, R_END)])
        f_state = ffn.take("f_state", [P, 2 * JF, 2 * NB + 2])
        f_taps = ffn.take("f_taps", [P, 2 * JF, 3])
        ext = [ffn.take(f"ext{n}", [P, CEXT]) for n in range(2)]
        cv = [ffn.take(f"cv{n}", [P, CEXT]) for n in range(2)]

        ps_out = ctx.enter_context(nc.psum_tensor("ps_out", [P, 4, 512], F32))
        ps_a = ctx.enter_context(nc.psum_tensor("ps_a", [P, 2, 512], F32))
        ps_b = ctx.enter_context(nc.psum_tensor("ps_b", [P, 2, 512], F32))
        b4, b5, b6, b7 = ps_a[:, 0, :], ps_a[:, 1, :], ps_b[:, 0, :], ps_b[:, 1, :]

        landed = [sem(f"landed{n}") for n in range(RING)]
        hi_ready = sem("hi_ready")
        lo_ready = sem("lo_ready")
        half_used = sem("half_used")
        evacuated = sem("evacuated")
        cst_in = sem("cst_in")
        mem_in = [sem(f"mem_in{n}") for n in range(4)]
        x_in = [sem(f"x_in{n}") for n in range(4)]
        x_back = [sem(f"x_back{n}") for n in range(4)]
        act_hi = sem("act_hi")
        act_lo = sem("act_lo")
        sq_done = sem("sq_done")
        sq_added = sem("sq_added")
        ssq = sem("ssq")
        root = sem("root")
        rstd_ready = sem("rstd_ready")
        mv_tr = sem("mv_tr")
        mv_ready = sem("mv_ready")
        f_ready = sem("f_ready")
        f_exp = sem("f_exp")
        f_exp1 = sem("f_exp1")
        f_log = sem("f_log")
        g_rows = sem("g_rows")
        g_exps = sem("g_exps")
        rows_out = sem("rows_out")
        g_tr = sem("g_tr")
        g_cols = sem("g_cols")
        smp_in = sem("smp_in")
        rows_in = sem("rows_in")
        c_in = sem("c_in")
        a_in = sem("a_in")
        ws_ready = sem("ws_ready")
        wp_in = sem("wp_in")
        ext_in = sem("ext_in")
        clamped = sem("clamped")
        decayed = sem("decayed")
        tok_tr = sem("tok_tr")
        k_copied = sem("k_copied")
        prods = sem("prods")
        updates = sem("updates")
        chained = sem("chained")
        sums = sem("sums")
        h_ready = sem("h_ready")
        h_sq = sem("h_sq")
        h_root = sem("h_root")
        o_gate = sem("o_gate")
        c_done = sem("c_done")
        c_out = sem("c_out")
        u_act = sem("u_act")
        v_act = sem("v_act")
        va_tr = sem("va_tr")
        va_copied = sem("va_copied")
        mixed = sem("mixed")
        a_done = sem("a_done")
        va_out = sem("va_out")
        pooled = sem("pooled")
        pool_out = sem("pool_out")
        b_done = sem("b_done")
        conv_in = sem("conv_in")
        conv_out = sem("conv_out")
        d_done = sem("d_done")
        kc_in = sem("kc_in")
        vc_in = sem("vc_in")
        pad_zero = sem("pad_zero")
        pad_ready = sem("pad_ready")
        scored = sem("scored")
        topped = sem("topped")
        exped = sem("exped")
        normed = sem("normed")
        turned = sem("turned")
        turn_a = sem("turn_a")
        turn_v = sem("turn_v")
        attended = sem("attended")
        o_hi_done = sem("o_hi_done")
        o_lo_done = sem("o_lo_done")
        fs_in = sem("fs_in")
        g_conv = sem("g_conv")
        g_silu = sem("g_silu")
        h_prod = sem("h_prod")
        h_hi_done = sem("h_hi_done")
        h_lo_done = sem("h_lo_done")
        y_done = sem("y_done")
        stored = sem("stored")
        dve_order = sem("dve_order")

        wall, x_d = ins["wall"], ins["x"]
        scratch = nc.dram_tensor("gate_rows", (H, 3, T), F32, kind="Internal").ap()

        K_MEM, K_MIX, K_Y, K_CROSS, K_FFN = [KD * n for n in range(5)]
        S_MEM, S_MIX, S_CROSS, S_FFN, S_FIN = range(5)

        def halves(ap):
            return ap.rearrange("p (a b) -> p a b", a=2)

        def out_view(o):
            q = o.mod(2)
            return ps_out[:, 2 * q:2 * q + 2, 0:TH]

        def out_bank(o, n):
            return ps_out[:, 2 * o.mod(2) + n, :]

        def smp(ap, before):
            return ap[:, before + SEQ:before + SEQ + NB * (before + NT)].rearrange("p (b t) -> p b t", t=before + NT)

        def by_smp(ap):
            return ap.rearrange("p (b t) -> p b t", t=NT)

        def eps(n=P):
            return cst[0:n, C_EPS:C_EPS + 1]

        block = ctx.enter_context(nc.Block())

        @block.sync
        def _(sp):
            for n in range(RING):
                sp.dma_start(w_raw[:, n, :], wall[n]).then_inc(landed[n], 16)
                if n == 0:
                    sp.dma_start(cst[:, :], ins["cst"]).then_inc(cst_in, 16)
                    sp.dma_start(vec[:, :], ins["vec"]).then_inc(cst_in, 16)
                sp.dma_start(m_raw[:, 4 * n:4 * n + 4, :], ins["mem"][:, 4 * n:4 * n + 4, :]).then_inc(mem_in[n], 16)
            for n in range(4):
                sp.dma_start(x_t[:, 4 * n:4 * n + 4, :], x_d[:, 4 * n:4 * n + 4, :]).then_inc(x_in[n], 16)
            with sp.Fori(1, N_UNITS // RING) as i:
                for j in range(RING):
                    sp.wait_ge(lo_ready, i * RING + (j - RING + 1))
                    sp.dma_start(w_raw[:, j, :], wall[i * RING + j]).then_inc(landed[j], 16)
            for n in range(N_UNITS // RING * RING, N_UNITS):
                sp.wait_ge(lo_ready, n - RING + 1)
                sp.dma_start(w_raw[:, n % RING, :], wall[n]).then_inc(landed[n % RING], 16)

        @block.gpsimd
        def _(pool):
            n_stored = [0]

            def store(dst, src):
                pool.dma_start(dst, src).then_inc(stored, 16)
                n_stored[0] += 16

            def squares(group, n):
                if group:
                    pool.wait_ge(ssq, group)
                for k in range(KD):
                    c = group * KD + k
                    pool.wait_ge(sq_done, c + 1)
                    if k == 0:
                        nc.gpsimd.tensor_copy(sq_sum[:, 0:n], sq_tmp[:, c % 2, 0:n]).then_inc(sq_added, 1)
                    else:
                        pool.wait_ge(sq_added, c)
                        nc.gpsimd.tensor_tensor(sq_sum[:, 0:n], sq_sum[:, 0:n], sq_tmp[:, c % 2, 0:n],
                                                ALU.add).then_inc(sq_added, 1)

            squares(S_MEM, NM)
            squares(S_MIX, T)
            pool.wait_ge(evacuated, O_MEM + H)
            store(outs["mem_k"], mk_t[:, :, :])
            pool.wait_ge(mv_ready, MT)
            store(outs["mem_v"], mv_t[:, :, :])
            pool.wait_ge(act_lo, K_Y)
            pool.wait_ge(act_hi, K_Y)
            pool.wait_ge(rstd_ready, S_MIX + 1)
            pool.dma_start(ms_in[:, :], ins["m_smp"]).then_inc(smp_in, 16)
            pool.wait_ge(g_exps, 3)
            pool.dma_start(scratch, r3[:, :, :]).then_inc(rows_out, 16)
            pool.dma_start(outs["m_all"], w_row[:, :]).then_inc(rows_out, 16)
            pool.wait_ge(rows_out, 32)
            pool.wait_ge(g_cols, 2)
            pool.dma_start(n_smp[:, :, :], ins["n_smp"]).then_inc(smp_in, 16)

            def head_loads(h, i):
                pool.dma_start(rows[:, :, :], scratch[h].partition_broadcast(P)).then_inc(rows_in, 16)
                pool.dma_start(c_smp[:, :, :], ins["c_smp"][h]).then_inc(c_in, 16)
                pool.dma_start(bs_t[:, :], ins["b_s"][h].partition_broadcast(P)).then_inc(a_in, 16)
                pool.dma_start(ws_t[:, :], ins["w_s"][h]).then_inc(a_in, 16)
                pool.dma_start(wd_t[:, :], ins["w_s_smp"][h]).then_inc(a_in, 16)
                pool.dma_start(smp(pe1, PST)[:, :, 0:PST], ins["pool_st"][h]).then_inc(ext_in, 16)
                pool.dma_start(wp_t[:, :], ins["w_pool"][h]).then_inc(wp_in, 16)
                pool.wait_ge(a_in, (i + 1).times(48).value())
                nc.gpsimd.tensor_tensor(ws_t[:, :], ws_t[:, :], cst[:, C_TRI:C_TRI + P],
                                        ALU.mult).then_inc(ws_ready, 1)
                nc.gpsimd.tensor_tensor(wd_t[:, :], wd_t[:, :], cst[0:NS, C_STRI:C_STRI + NS],
                                        ALU.mult).then_inc(ws_ready, 1)

            def head_stores(h, i):
                pool.wait_ge(v_act, (i + 1).value())
                pool.dma_start(outs["v_rows"][h], va_t[:, SEQ:T]).then_inc(va_out, 16)
                pool.wait_ge(pooled, (i + 1).value())
                pool.dma_start(outs["pool_p"][h], pe1[:, SEQ:SEQ + PST]).then_inc(pool_out, 16)
                pool.dma_start(outs["pool_s"][h], smp(pe1, PST)[:, :, NT:NT + PST]).then_inc(pool_out, 16)
                pool.wait_ge(chained, (i + 1).times(2).value())
                pool.dma_start(outs["c_p"][h], state[:, CH - 1, :]).then_inc(c_out, 16)
                pool.dma_start(outs["n_s"][h], n_smp[:, h, :]).then_inc(c_out, 16)
                pool.dma_start(outs["c_s"][h], c_smp[:, :, :]).then_inc(c_out, 16)
                pool.wait_ge(pool_out, (i + 1).times(32).value())
                pool.dma_start(smp(dx_e, 2)[:, :, 0:2], ins["conv_st"][h]).then_inc(conv_in, 16)
                pool.wait_ge(d_done, (i + 1).value())
                pool.dma_start(outs["conv_p"][h], dx_e[:, SEQ:SEQ + 2]).then_inc(conv_out, 16)
                pool.dma_start(outs["conv_s"][h], smp(dx_e, 2)[:, :, NT:NT + 2]).then_inc(conv_out, 16)
                pool.wait_ge(c_done, (i + 1).value())
                pool.wait_ge(a_done, (i + 1).value())
                pool.wait_ge(b_done, (i + 1).value())
                pool.wait_ge(c_out, (i + 1).times(48).value())
                pool.wait_ge(va_out, (i + 1).times(16).value())
                pool.wait_ge(conv_out, (i + 1).times(32).value())

            head_loads(0, Index(0))
            with pool.Fori(0, H - 1) as h:
                head_stores(h, Index(0, h, 1))
                head_loads(h + 1, Index(1, h, 1))
            head_stores(H - 1, Index(H - 1))
            for n in range(4):
                pool.dma_start(x_t[:, 4 * n:4 * n + 4, :], x_d[:, 4 * n:4 * n + 4, :]).then_inc(x_back[n], 16)
            pool.wait_ge(act_lo, K_CROSS)
            pool.wait_ge(act_hi, K_CROSS)
            pool.dma_start(kc_t[:, :, :, :], ins["k_cache"]).then_inc(kc_in, 16)
            squares(S_CROSS, T)
            pool.wait_ge(half_used, 2 * U_O)
            nc.gpsimd.memset(q_pad[:, :, :, :], 0.0).then_inc(pad_zero, 1)
            pool.dma_start(vc_t[:, :, :, :], ins["v_cache"]).then_inc(vc_in, 16)
            pool.wait_ge(attended, CH + 1)
            pool.wait_ge(stored, 32)
            pool.dma_start(f_state[:, :, 0:2 * NB], ins["ffn_st"]).then_inc(fs_in, 16)
            pool.dma_start(f_taps[:, :, :], ins["w_fconv"]).then_inc(fs_in, 16)
            squares(S_FFN, T)
            squares(S_FIN, T)
            store(outs["ffn_st"], f_state[:, :, :])
            for k in range(KD):
                pool.wait_ge(y_done, k + 1)
                store(outs["y"][:, k, :], x_t[:, k, :])
            pool.wait_ge(stored, n_stored[0])
            pool.wait_ge(rows_out, 32)
            pool.wait_ge(c_out, 48 * H)
            pool.wait_ge(va_out, 16 * H)
            pool.wait_ge(pool_out, 32 * H)
            pool.wait_ge(conv_out, 32 * H)

        @block.scalar
        def _(act):
            def split_hi(n):
                s = n.mod(RING)
                act.wait_ge(landed[s], (n.over(RING) + 1).times(16).value())
                if n.reg is not None or n.const >= RING:
                    act.wait_ge(half_used, (n - (RING - 1)).times(2).value())
                nc.scalar.activation(w_hi[:, s, :], w_raw[:, s, :], ACT.Copy).then_inc(hi_ready, 1)

            def splits(u, n=2):
                for k in range(n):
                    if u.reg is not None or u.const + 2 + k < N_UNITS:
                        split_hi(u + 2 + k)

            def square(c, src, n=T):
                if c >= 2:
                    act.wait_ge(sq_added, c - 1)
                nc.scalar.activation(sq_tmp[:, c % 2, 0:n], src, ACT.Square).then_inc(sq_done, 1)

            def rms_root(group, dst, n=T):
                act.wait_ge(ssq, group + 1)
                nc.scalar.activation(halves(dst), ps_b[:, :, 0:n // 2], ACT.Sqrt, bias=eps(),
                                     scale=1.0 / D).then_inc(root, 1)

            def act_chunks(u, src, dst, gain=None):
                for k in range(KD):
                    scale = 1.0 if gain is None else vec[:, gain + k:gain + k + 1]
                    nc.scalar.activation(dst[:, k, :], src[:, k, :], ACT.Copy, scale=scale).then_inc(act_hi, 1)
                    if k % 8 == 7:
                        split_hi(Index(u + 2 + k // 8))

            split_hi(Index(0))
            split_hi(Index(1))
            act.wait_ge(cst_in, 32)
            for k in range(KD):
                if k % 4 == 0:
                    act.wait_ge(mem_in[k // 4], 16)
                nc.scalar.activation(m_hi[:, k, :], m_raw[:, k, :], ACT.Copy,
                                     scale=vec[:, V_MEM + k:V_MEM + k + 1]).then_inc(act_hi, 1)
                square(k, m_raw[:, k, :], NM)
                if k % 8 == 7:
                    split_hi(Index(2 + k // 8))
            done = 0
            for o in range(1, 8):
                splits(Index(U_MEM + 2 * o))
                if o == 1:
                    rms_root(S_MEM, rstd_m, NM)
                for k in range(done, min(done + 3, KD)):
                    if k % 4 == 0:
                        act.wait_ge(x_in[k // 4], 16)
                    nc.scalar.activation(a_hi[:, k, :], x_t[:, k, :], ACT.Copy,
                                         scale=vec[:, V_MIX + k:V_MIX + k + 1]).then_inc(act_hi, 1)
                    square(S_MIX * KD + k, x_t[:, k, :])
                done = min(done + 3, KD)
            splits(Index(U_GATE))
            act.wait_ge(mv_tr, 1)
            for m in range(MT):
                nc.scalar.activation(mv_t[:, m, :], ps_a[:, m, :], ACT.Copy).then_inc(mv_ready, 1)
            rms_root(S_MIX, rstd[:, :])

            def o_or_u(j):
                act.wait_ge(evacuated, O_PRE + j + 1)
                if j < H:
                    nc.scalar.activation(y_t[:, 2 * H + j, :], y_t[:, 2 * H + j, :], ACT.Sigmoid).then_inc(o_gate, 1)
                else:
                    nc.scalar.activation(y_t[:, j - H, :], y_t[:, j - H, :], ACT.Gelu_apprx_tanh).then_inc(u_act, 1)

            splits(Index(U_PRE))
            act.wait_ge(f_ready, 1)
            nc.scalar.activation(m_row[:, :], f_row[:, :], ACT.Exp).then_inc(f_exp, 1)
            act.wait_ge(f_exp1, 1)
            nc.scalar.activation(w_row[:, :], m_row[:, :], ACT.Ln).then_inc(f_log, 1)
            for j in range(1, 5):
                splits(Index(U_PRE + 2 * j))
                o_or_u(j - 1)
            act.wait_ge(g_rows, 1)
            nc.scalar.activation(r3[:, 1, :], r3[:, 1, :], ACT.Exp, scale=-1.0).then_inc(g_exps, 1)
            nc.scalar.activation(r3[:, 2, :], w_row[:, :], ACT.Exp, scale=-1.0).then_inc(g_exps, 1)
            nc.scalar.activation(b_row[:, :], b_row[:, :], ACT.Exp).then_inc(g_exps, 1)
            for j in range(5, 8):
                splits(Index(U_PRE + 2 * j))
                o_or_u(j - 1)
            act.wait_ge(g_tr, 1)
            act.wait_ge(rows_out, 32)
            by_tok = b4[:, 0:2 * (CH + 1) * H].rearrange("p (q c h) -> p q c h", q=2, h=H)
            nc.scalar.activation(cols[:, :, 0:CH, :], by_tok[:, :, 0:CH, :], ACT.Copy).then_inc(g_cols, 1)
            nc.scalar.activation(cols[0:NS, :, CH, :], by_tok[0:NS, :, CH, :], ACT.Copy).then_inc(g_cols, 1)
            o_or_u(7)
            with act.Fori(0, H) as h:
                i = Index(0, h, 1)

                def slot(j):
                    splits(Index(U_MIX + 2 * j, h, 2 * PAN))

                slot(0)
                slot(1)
                slot(2)
                slot(3)
                act.wait_ge(clamped, (i + 1).value())
                nc.scalar.activation(dmat[:, :, :], dmat[:, :, :], ACT.Exp).then_inc(decayed, 1)
                nc.scalar.activation(dmat_s[:, :], dmat_s[:, :], ACT.Exp).then_inc(decayed, 1)
                slot(4)
                act.wait_ge(tok_tr, (i + 1).value())
                for c in range(CH):
                    nc.scalar.activation(k_tok[:, c, :], b4[:, P * c:P * c + P], ACT.Copy,
                                         scale=cols[:, 1, c, bass.ds(h, 1)]).then_inc(k_copied, 1)
                nc.scalar.activation(k_tok[0:NS, CH, :], b6[0:NS, 0:P], ACT.Copy,
                                     scale=cols[0:NS, 1, CH, bass.ds(h, 1)]).then_inc(k_copied, 1)
                act.wait_ge(evacuated, (i.times(PAN) + O_MIX + 4).value())
                nc.scalar.activation(va_t[:, :], va_t[:, :], ACT.Gelu_apprx_tanh).then_inc(v_act, 1)
                slot(5)
                slot(6)
                act.wait_ge(h_ready, (i + 1).value())
                nc.scalar.activation(q_in[:, :], h_t, ACT.Square).then_inc(h_sq, 1)
                slot(7)
                act.wait_ge(va_tr, (i + 1).value())
                nc.scalar.activation(va_tok[:, 0:CH, :].rearrange("p c d -> p (c d)"), b4, ACT.Copy).then_inc(va_copied, 1)
                nc.scalar.activation(va_tok[0:NS, CH, :], b5[0:NS, 0:P], ACT.Copy).then_inc(va_copied, 1)
                nc.scalar.activation(q_in[:, 0:SEQ], b7, ACT.Sqrt, bias=eps(), scale=1.0 / P).then_inc(h_root, 1)
                nc.scalar.activation(q_in[:, SEQ:T], b6[:, 0:NS], ACT.Sqrt, bias=eps(), scale=1.0 / P).then_inc(h_root, 1)
            act.wait_ge(half_used, 2 * U_OUT)
            act.wait_ge(d_done, H)
            act.wait_ge(c_done, H)
            act.wait_ge(b_done, H)
            act.wait_ge(a_done, H)
            act_chunks(U_OUT, y_t, a_hi)
            for m in range(KD):
                if m:
                    splits(Index(U_OUT + 2 * m))
                act.wait_ge(evacuated, O_OUT + m + 1)
                square(S_CROSS * KD + m, x_t[:, m, :])
            act_chunks(U_Q, x_t, a_hi, V_CROSS)
            for m in range(1, H):
                splits(Index(U_Q + 2 * m))
                if m == 1:
                    rms_root(S_CROSS, rstd[:, :])
            for i in range(CH + 1):
                r = P if i < CH else NS
                act.wait_ge(topped, i + 1)
                if i:
                    act.wait_ge(turned, i)
                for h in range(H):
                    nc.scalar.activation(prob[0:r, h, :], ps_a[0:r, h // 2, h % 2 * NM:(h % 2 + 1) * NM], ACT.Exp,
                                         bias=neg_top[0:r, h:h + 1], scale=SCALE,
                                         accum_out=p_sum[0:r, h:h + 1]).then_inc(exped, 1)
                act.wait_ge(turned, i + 1)
                nc.scalar.activation(prob_t[:, 0:4, 0:r], b6.rearrange("p (n t) -> p n t", n=4)[:, :, 0:r],
                                     ACT.Copy).then_inc(turn_a, 1)
                act.wait_ge(attended, i + 1)
                nc.scalar.activation(o_hi[:, :, P * i:P * i + r], b4.rearrange("p (n t) -> p n t", n=4)[:, :, 0:r],
                                     ACT.Copy).then_inc(o_hi_done, 1)
            for m in range(KD):
                if m % 2 == 0:
                    splits(Index(U_O + m // 2), 1)
                act.wait_ge(evacuated, O_O + m + 1)
                square(S_FFN * KD + m, x_t[:, m, :])
            act_chunks(U_FFN, x_t, a_hi, V_FFN)

            def hidden(u0, j, c, first):
                if not (first and j == 0):
                    splits(u0 + 4 * j)
                if first and j == 0:
                    rms_root(S_FFN, rstd[:, :])
                act.wait_ge(g_conv, (c + 1).value())
                nc.scalar.activation(cv[0][:, 0:CEXT - 2], cv[0][:, 0:CEXT - 2], ACT.Silu).then_inc(g_silu, 1)
                splits(u0 + 4 * j + 2)
                act.wait_ge(h_prod, (c + 1).value())
                nc.scalar.activation(h_hi[:, j, 0:SEQ], cv[0][:, 0:SEQ], ACT.Copy).then_inc(h_hi_done, 1)
                nc.scalar.activation(by_smp(h_hi[:, j, SEQ:T]), smp(cv[0], 2)[:, :, 0:NT], ACT.Copy).then_inc(h_hi_done, 1)

            def group(u0, c0, first=False):
                for j in range(GRP):
                    hidden(u0, j, c0 + j, first)
                for m in range(KD):
                    splits(u0 + 4 * GRP + m, 1)

            group(Index(U_FFN), Index(0), first=True)
            with act.Fori(1, NG) as g:
                group(Index(U_FFN, g, FU), Index(0, g, GRP))
            for j in range(REST):
                hidden(Index(U_LAST), j, Index(NG * GRP + j), False)
            for m in range(KD):
                if m % 2 == 0:
                    splits(Index(U_LDN + m // 2), 1)
                act.wait_ge(evacuated, O_LDN + m + 1)
                square(S_FIN * KD + m, x_t[:, m, :])
            rms_root(S_FIN, rstd[:, :])

        @block.tensor
        def _(pe):
            def ident(n=P):
                return cst[0:n, C_ID:C_ID + n]

            def ones(n=P, m=P):
                return cst[0:n, C_ONE:C_ONE + m]

            def blocks(o, u, pairs, hi, lo, n, wait_chunk=None, chunk_each=1):
                s = u.mod(RING)
                pe.wait_ge(hi_ready, (u + 1).value())
                pe.wait_ge(lo_ready, (u + 1).value())
                for b, c, first, last, ends in pairs:
                    if wait_chunk is not None:
                        wait_chunk(c)
                    wh, wl = w_hi[:, s, P * b:P * b + P], w_lo[:, s, P * b:P * b + P]
                    terms = [(wh, hi), (wh, lo), (wl, hi)]
                    for t, (w, a) in enumerate(terms):
                        for k, m in enumerate(range(0, n[0] * n[1], n[1])):
                            ins_ = nc.tensor.matmul(out_bank(o, k)[:, 0:n[1]], w, a[:, c, m:m + n[1]],
                                                    start=first and t == 0, stop=last and t == 2)
                    if ends:
                        ins_.then_inc(half_used, 1)

            def free(o):
                if o.reg is not None or o.const >= 2:
                    pe.wait_ge(evacuated, (o - 1).value())

            def output(o, u, hi, lo, n=(2, TH), wait_chunk=None):
                free(o)
                for v in range(2):
                    pairs = [(b, UB * v + b, v == 0 and b == 0, v == 1 and b == UB - 1, b % 4 == 3)
                             for b in range(UB)]
                    blocks(o, u + v, pairs, hi, lo, n, wait_chunk)

            def chunk_waits(k0):
                def wait(c):
                    pe.wait_ge(act_hi, k0 + c + 1)
                    pe.wait_ge(act_lo, k0 + c + 1)
                return wait

            def sum_squares(group, n=T):
                pe.wait_ge(sq_added, (group + 1) * KD)
                for k in range(2):
                    m = nc.tensor.matmul(ps_b[:, k, 0:n // 2], ones(), sq_sum[:, k * n // 2:(k + 1) * n // 2],
                                         start=True, stop=True)
                m.then_inc(ssq, 1)

            pe.wait_ge(cst_in, 32)
            for o in range(8):
                output(Index(O_MEM + o), Index(U_MEM + 2 * o), m_hi, m_lo, (1, NM),
                       chunk_waits(K_MEM) if o == 0 else None)
                if o == 0:
                    sum_squares(S_MEM, NM)
            output(Index(O_GATE), Index(U_GATE), a_hi, a_lo, wait_chunk=chunk_waits(K_MIX))
            pe.wait_ge(evacuated, O_MEM + 8)
            for h in range(H):
                for m in range(MT):
                    t = nc.tensor.transpose(ps_a[:, m, P * h:P * h + P], vt_mem[:, h, P * m:P * m + P], ident())
            t.then_inc(mv_tr, 1)
            pe.wait_ge(root, S_MEM + 1)
            sum_squares(S_MIX)

            def gates_by_token():
                pe.wait_ge(g_exps, 3)
                pe.wait_ge(mv_ready, MT)
                for q, row in enumerate((a_row, b_row)):
                    for c in range(CH + 1):
                        r = P if c < CH else NS
                        n = (q * (CH + 1) + c) * H
                        t = nc.tensor.transpose(b4[0:r, n:n + H], row[:, P * c:P * c + r], ident(H))
                t.then_inc(g_tr, 1)

            def head(h, i):
                def slot(j):
                    output(i.times(PAN) + (O_MIX + j), i.times(2 * PAN) + (U_MIX + 2 * j), a_hi, a_lo)

                slot(0)
                slot(1)
                slot(2)
                slot(3)
                pe.wait_ge(evacuated, (i.times(PAN) + O_MIX + 3).value())
                for c in range(CH):
                    nc.tensor.transpose(b4[:, P * c:P * c + P], qkv[:, 1, P * c:P * c + P], ident())
                    nc.tensor.transpose(b5[:, P * c:P * c + P], qkv[:, 2, P * c:P * c + P], ident())
                    nc.tensor.matmul(b7[:, P * c:P * c + P], qkv[:, 1, P * c:P * c + P], qkv[:, 0, P * c:P * c + P],
                                     start=True, stop=True)
                nc.tensor.transpose(b6[0:NS, 0:P], qkv[:, 1, SEQ:T], ident())
                nc.tensor.transpose(b6[0:NS, P:2 * P], qkv[:, 2, SEQ:T], ident())
                nc.tensor.matmul(b6[0:NS, 2 * P:2 * P + NS], qkv[:, 1, SEQ:T], qkv[:, 0, SEQ:T],
                                 start=True, stop=True).then_inc(tok_tr, 1)
                slot(4)
                pe.wait_ge(k_copied, (i + 1).times(CH + 1).value())
                pe.wait_ge(prods, (i + 1).value())
                pe.wait_ge(c_in, (i + 1).times(16).value())
                for c in range(CH):
                    nc.tensor.matmul(b4[:, P * c:P * c + P], k_tok[:, c, :], v_tok[:, c, :], start=True, stop=True)
                    nc.tensor.matmul(b7[:, c:c + 1], k_tok[:, c, :], ones(P, 1), start=True, stop=True)
                nc.tensor.matmul(b7[:, CH:CH + NB], k_tok[0:NS, CH, :], cst[0:NS, C_BLK:C_BLK + NB],
                                 start=True, stop=True)
                nc.tensor.matmul(b6, k_tok[0:NS, CH, :], vws[0][0:NS, :], start=True, stop=True)
                nc.tensor.matmul(b5[:, 64:64 + NS], ones(NS), dmat_s[:, :], start=True, stop=False)
                nc.tensor.matmul(b5[:, 64:64 + NS], ones(), nq[:, :], start=False, stop=True)
                for b in range(NB):
                    t0 = NT * b
                    nc.tensor.matmul(b5[:, t0:t0 + NT], c_smp[:, b, :], q_in[:, SEQ + t0:SEQ + t0 + NT],
                                     start=b == 0, stop=False, skip_group_check=True)
                nc.tensor.matmul(b5[:, 0:NS], v_tok[0:NS, CH, :], dmat_s[:, :], start=False, stop=True,
                                 skip_group_check=True).then_inc(updates, 1)
                slot(5)
                pe.wait_ge(chained, (i.times(2) + 1).value())
                for c in range(CH):
                    m = nc.tensor.matmul(b4[:, P * c:P * c + P], v_tok[:, c, :], dmat[:, c, :],
                                         start=True, stop=c == 0)
                    if c:
                        m = nc.tensor.matmul(b4[:, P * c:P * c + P], state[:, c - 1, 0:P], q_in[:, P * c:P * c + P],
                                             start=False, stop=True)
                nc.tensor.matmul(b7, ones(), den_t, start=True, stop=True)
                nc.tensor.matmul(b6, k_tok[0:NS, CH, :], vws[1][0:NS, :], start=True, stop=True).then_inc(sums, 1)
                slot(6)
                pe.wait_ge(h_sq, (i + 1).value())
                pe.wait_ge(chained, (i + 1).times(2).value())
                nc.tensor.matmul(b7, ones(), q_in[:, 0:SEQ], start=True, stop=True)
                nc.tensor.matmul(b6[:, 0:NS], ones(), q_in[:, SEQ:T], start=True, stop=True)
                pe.wait_ge(v_act, (i + 1).value())
                for c in range(CH):
                    nc.tensor.transpose(b4[:, P * c:P * c + P], va_t[:, P * c:P * c + P], ident())
                nc.tensor.transpose(b5[0:NS, 0:P], va_t[:, SEQ:T], ident()).then_inc(va_tr, 1)
                slot(7)
                pe.wait_ge(va_copied, (i + 1).times(2).value())
                pe.wait_ge(ws_ready, (i + 1).times(2).value())
                for c in range(CH):
                    nc.tensor.matmul(b4[:, P * c:P * c + P], va_tok[:, c, :], ws_t[:, :], start=True, stop=True)
                nc.tensor.matmul(b5[:, 0:NS], va_tok[0:NS, CH, :], wd_t[:, :], start=True, stop=True)
                pe.wait_ge(h_root, (i + 1).times(2).value())
                pe.wait_ge(pooled, (i + 1).value())
                pe.wait_ge(wp_in, (i + 1).times(16).value())
                nc.tensor.matmul(b6[:, 0:TH], wp_t[:, :], y_t[:, H + h, 0:TH], start=True, stop=True)
                nc.tensor.matmul(b7[:, 0:TH], wp_t[:, :], y_t[:, H + h, TH:T], start=True, stop=True).then_inc(mixed, 1)

            for j in range(2 * H):
                output(Index(O_PRE + j), Index(U_PRE + 2 * j), a_hi, a_lo)
                if j == 6:
                    gates_by_token()
            with pe.Fori(0, H) as h:
                head(h, Index(0, h, 1))
            output(Index(O_OUT), Index(U_OUT), a_hi, a_lo, wait_chunk=chunk_waits(K_Y))
            output(Index(O_OUT + 1), Index(U_OUT + 2), a_hi, a_lo)
            with pe.Fori(1, KD // 2) as m:
                for j in range(2):
                    output(Index(O_OUT + j, m, 2), Index(U_OUT + 2 * j, m, 4), a_hi, a_lo)
            output(Index(O_Q), Index(U_Q), a_hi, a_lo, wait_chunk=chunk_waits(K_CROSS))
            pe.wait_ge(a_done, H)
            pe.wait_ge(b_done, H)
            sum_squares(S_CROSS)
            for m in range(1, H):
                output(Index(O_Q + m), Index(U_Q + 2 * m), a_hi, a_lo)
            pe.wait_ge(evacuated, O_Q + H)
            pe.wait_ge(root, S_CROSS + 1)
            for i in range(CH + 1):
                r = P if i < CH else NS
                if i:
                    pe.wait_ge(o_lo_done, i)
                if i < CH:
                    for h in range(H):
                        s_m = nc.tensor.matmul(ps_a[:, h // 2, h % 2 * NM:(h % 2 + 1) * NM], q_t[:, h, P * i:P * i + P],
                                               mk_t[:, h, :], start=True, stop=True)
                else:
                    pe.wait_ge(pad_ready, 1)
                    pe.wait_ge(kc_in, 16)
                    for h in range(H):
                        for b in range(NB):
                            s_m = nc.tensor.matmul(ps_a[0:NS, h // 2, h % 2 * NM:(h % 2 + 1) * NM], q_pad[:, h, b, :],
                                                   kc_t[:, h, b, :], start=b == 0, stop=b == NB - 1)
                s_m.then_inc(scored, 1)
                pe.wait_ge(normed, i + 1)
                if i:
                    pe.wait_ge(turn_v, i)
                for h in range(H):
                    for m in range(MT):
                        n = h * MT + m
                        s_m = nc.tensor.transpose(ps_b[:, n // 4, n % 4 * P:n % 4 * P + r], prob[0:r, h, P * m:P * m + P],
                                                  ident(r))
                s_m.then_inc(turned, 1)
                pe.wait_ge(turn_a, i + 1)
                pe.wait_ge(turn_v, i + 1)
                if i < CH:
                    for h in range(H):
                        for m in range(MT):
                            s_m = nc.tensor.matmul(b4[:, P * h:P * h + P], mv_t[:, m, P * h:P * h + P],
                                                   prob_t[:, h * MT + m, :], start=m == 0, stop=m == MT - 1)
                else:
                    pe.wait_ge(vc_in, 16)
                    for h in range(H):
                        for b in range(NB):
                            for m in range(MT):
                                s_m = nc.tensor.matmul(b4[:, P * h + NT * b:P * h + NT * b + NT],
                                                       vc_t[:, b, m, P * h:P * h + P],
                                                       prob_t[:, h * MT + m, NT * b:NT * b + NT],
                                                       start=m == 0, stop=m == MT - 1)
                s_m.then_inc(attended, 1)
            pe.wait_ge(o_hi_done, CH + 1)
            pe.wait_ge(o_lo_done, CH + 1)
            for m in range(KD):
                free(Index(O_O + m))
                a = 4 * (m % 2)
                blocks(Index(O_O + m), Index(U_O + m // 2), [(a + c, c, c == 0, c == H - 1, c == H - 1) for c in range(H)],
                       o_hi, o_lo, (2, TH))
            output(Index(O_FFN), Index(U_FFN), a_hi, a_lo, wait_chunk=chunk_waits(K_FFN))
            sum_squares(S_FFN)

            def hidden_waits(c0):
                def wait(c):
                    pe.wait_ge(h_hi_done, (c0 + c + 1).times(2).value())
                    pe.wait_ge(h_lo_done, (c0 + c + 1).times(2).value())
                return wait

            def group(u0, o0, c0, first=0):
                for j in range(first, 2 * GRP):
                    output(o0 + j, u0 + 2 * j, a_hi, a_lo)
                for m in range(KD):
                    free(o0 + 2 * GRP + m)
                    blocks(o0 + 2 * GRP + m, u0 + 4 * GRP + m, [(b, b, b == 0, b == GRP - 1, b % 4 == 3) for b in range(GRP)],
                           h_hi, h_lo, (2, TH), hidden_waits(c0) if m == 0 else None)

            group(Index(U_FFN), Index(O_FFN), Index(0), first=1)
            with pe.Fori(1, NG) as g:
                group(Index(U_FFN, g, FU), Index(O_FFN, g, FO), Index(0, g, GRP))
            for j in range(2 * REST):
                output(Index(O_LAST + j), Index(U_LAST + 2 * j), a_hi, a_lo)
            for m in range(KD):
                free(Index(O_LDN + m))
                a = REST * (m % 2)
                blocks(Index(O_LDN + m), Index(U_LDN + m // 2),
                       [(a + c, c, c == 0, c == REST - 1, c == REST - 1) for c in range(REST)], h_hi, h_lo, (2, TH),
                       hidden_waits(Index(NG * GRP)) if m == 0 else None)
            sum_squares(S_FIN)

        @block.vector
        def _(dve):
            tt, ts, stt = nc.vector.tensor_tensor, nc.vector.tensor_scalar, nc.vector.scalar_tensor_tensor
            copy = nc.vector.tensor_copy
            link = Chain(dve, dve_order)

            def splits(u, n=2):
                for k in range(2, n + 2):
                    if u.reg is None and u.const + k >= N_UNITS:
                        continue
                    s = (u + k).mod(RING)
                    dve.wait_ge(hi_ready, (u + k + 1).value())
                    tt(w_lo[:, s, :], w_raw[:, s, :], w_hi[:, s, :], ALU.subtract).then_inc(lo_ready, 1)

            def chunk_lo(count, dst, src, hi, gain=None):
                dve.wait_ge(act_hi, count + 1)
                if gain is None:
                    tt(dst, src, hi, ALU.subtract).then_inc(act_lo, 1)
                else:
                    stt(dst, src, vec[:, gain:gain + 1], hi, ALU.mult, ALU.subtract).then_inc(act_lo, 1)

            def act_chunks(u, k0, src, gain=None):
                for k in range(KD):
                    chunk_lo(k0 + k, a_lo[:, k, :], src[:, k, :], a_hi[:, k, :], None if gain is None else gain + k)
                    if k % 8 == 7:
                        splits(Index(u + k // 8), 1)

            def inv_root(group, r):
                dve.wait_ge(root, group + 1)
                nc.vector.reciprocal(r, r).then_inc(rstd_ready, 1)
                dve.wait_ge(rstd_ready, group + 1)

            def summed(u):
                dve.wait_ge(half_used, (u + 1).times(2).value())

            def evac(o, u, dst):
                summed(u)
                tt(halves(dst), out_view(o), halves(rstd[:, :]), ALU.mult).then_inc(evacuated, 1)

            def evac_ext(o, u, dst, before):
                summed(u)
                tt(dst[:, before:before + TH], out_bank(o, 0)[:, 0:TH], rstd[:, 0:TH], ALU.mult)
                tt(dst[:, before + TH:before + SEQ], out_bank(o, 1)[:, 0:SEQ - TH], rstd[:, TH:SEQ], ALU.mult)
                tt(smp(dst, before)[:, :, before:before + NT], by_smp(out_bank(o, 1)[:, SEQ - TH:TH]),
                   by_smp(rstd[:, SEQ:T]), ALU.mult).then_inc(evacuated, 1)
                dve.wait_ge(evacuated, (o + 1).value())

            def add_to_x(o, m):
                tt(halves(x_t[:, m, :]), out_view(o), halves(x_t[:, m, :]), ALU.add).then_inc(evacuated, 1)

            def conv3(dst, src, taps):
                n = CEXT - 2
                link(ts(dst[:, 0:n], src[:, 0:n], taps(0), None, ALU.mult))
                link(stt(dst[:, 0:n], src[:, 1:n + 1], taps(1), dst[:, 0:n], ALU.mult, ALU.add))
                return stt(dst[:, 0:n], src[:, 2:n + 2], taps(2), dst[:, 0:n], ALU.mult, ALU.add)

            splits(Index(-2), 2)
            dve.wait_ge(cst_in, 32)
            for k in range(KD):
                chunk_lo(K_MEM + k, m_lo[:, k, :], m_raw[:, k, :], m_hi[:, k, :], V_MEM + k)
                if k % 8 == 7:
                    splits(Index(k // 8), 1)
            dve.wait_ge(sq_done, KD)
            inv_root(S_MEM, rstd_m)
            done = 0
            for o in range(8):
                u = U_MEM + 2 * o
                if o:
                    splits(Index(u))
                    for k in range(done, min(done + 3, KD)):
                        chunk_lo(K_MIX + k, a_lo[:, k, :], x_t[:, k, :], a_hi[:, k, :], V_MIX + k)
                    done = min(done + 3, KD)
                summed(Index(u + 1))
                dst = mk_t[:, o, :] if o < H else vt_mem[:, o - H, :]
                tt(dst, out_bank(Index(o), 0)[:, 0:NM], rstd_m, ALU.mult).then_inc(evacuated, 1)

            def scan(bufs, pad, shifts, op):
                a, b = bufs
                for s in shifts:
                    n = a.shape[2]
                    link(tt(b[:, :, pad:n], a[:, :, pad:n], a[:, :, pad - s:n - s], op))
                    a, b = b, a
                return a[:, :, pad:n]

            def by_chunk(row):
                return row.rearrange("p (c t) -> p c t", t=P)

            SHIFTS_P, SHIFTS_S = [1 << n for n in range(7)], [1, 2]

            def gates_1():
                dve.wait_ge(mv_ready, MT)
                for b in scan_p:
                    nc.vector.memset(b[:, :, 0:P // 2], 0.0)
                for b in scan_s:
                    nc.vector.memset(b[:, :, 0:2], 0.0)
                dve.wait_ge(evacuated, O_GATE + 1)
                link(ts(gate[:, :], gate[:, :], vec[:, V_BG:V_BG + 1], None, ALU.add))
                link(copy(b_row[:, :], gate[32:32 + H, :]))
                stt(f_row[:, :], b_row[:, :], -1.0, b_row[:, :], ALU.mult, ALU.min).then_inc(f_ready, 1)
                dve.wait_ge(f_exp, 1)
                ts(m_row[:, :], m_row[:, :], 1.0, None, ALU.add).then_inc(f_exp1, 1)

            def gates_2():
                dve.wait_ge(f_log, 1)
                lp, ls = scan_p[0][:, :, P // 2:], scan_s[0][:, :, 2:]
                stt(lp, by_chunk(b_row[:, 0:SEQ]), 0.0, by_chunk(w_row[:, 0:SEQ]), ALU.min, ALU.subtract)
                link(stt(ls, by_smp(b_row[:, SEQ:T]), 0.0, by_smp(w_row[:, SEQ:T]), ALU.min, ALU.subtract))
                bp = scan(scan_p, P // 2, SHIFTS_P, ALU.add)
                bs = scan(scan_s, 2, SHIFTS_S, ALU.add)
                copy(by_chunk(b_row[:, 0:SEQ]), bp)
                link(copy(by_smp(b_row[:, SEQ:T]), bs))
                link(tt(a_row[:, :], gate[0:H, :], b_row[:, :], ALU.subtract))

            def gates_3():
                for b in scan_p:
                    nc.vector.memset(b[:, :, 0:P // 2], -3.0e38)
                for b in scan_s:
                    nc.vector.memset(b[:, :, 0:2], -3.0e38)
                copy(scan_p[0][:, :, P // 2:], by_chunk(a_row[:, 0:SEQ]))
                link(copy(scan_s[0][:, :, 2:], by_smp(a_row[:, SEQ:T])))
                top_p = scan(scan_p, P // 2, SHIFTS_P, ALU.max)
                top_s = scan(scan_s, 2, SHIFTS_S, ALU.max)
                link(nc.vector.memset(m_prev[:, 0:1], 0.0))
                for c in range(CH):
                    t1 = P * c + P
                    link(ts(m_row[:, P * c:t1], top_p[:, c, :], m_prev[:, c:c + 1], None, ALU.max))
                    if c < CH - 1:
                        link(tt(m_prev[:, c + 1:c + 2], b_row[:, t1 - 1:t1], m_row[:, t1 - 1:t1], ALU.add))
                dve.wait_ge(smp_in, 16)
                link(tt(by_smp(m_row[:, SEQ:T]), top_s, ms_in[:, :].unsqueeze(2).broadcast_to([H, NB, NT]), ALU.max))

            def gates_4():
                m_p, m_s = by_chunk(m_row[:, 0:SEQ]), by_smp(m_row[:, SEQ:T])
                ts(r3[:, 0, :], m_row[:, :], -1.0, None, ALU.mult)
                tt(by_chunk(r3[:, 1, 0:SEQ]), m_p, m_prev[:, :].unsqueeze(2).broadcast_to([H, CH, P]), ALU.subtract)
                tt(by_smp(r3[:, 1, SEQ:T]), m_s, ms_in[:, :].unsqueeze(2).broadcast_to([H, NB, NT]), ALU.subtract)
                link(tt(w_row[:, :], b_row[:, :], m_row[:, :], ALU.add))
                tt(by_chunk(b_row[:, 0:SEQ]), by_chunk(a_row[:, 0:SEQ]), m_p[:, :, P - 1:P].broadcast_to([H, CH, P]),
                   ALU.subtract)
                tt(by_smp(b_row[:, SEQ:T]), by_smp(a_row[:, SEQ:T]), m_s[:, :, NT - 1:NT].broadcast_to([H, NB, NT]),
                   ALU.subtract).then_inc(g_rows, 1)

            splits(Index(U_GATE))
            inv_root(S_MIX, rstd[:, :])
            evac(Index(O_GATE), Index(U_GATE + 1), gate[:, :])
            steps = [gates_2, gates_3, gates_4]
            splits(Index(U_PRE))
            gates_1()
            for j in range(2 * H):
                if j:
                    splits(Index(U_PRE + 2 * j))
                evac(Index(O_PRE + j), Index(U_PRE + 2 * j + 1), y_t[:, 2 * H + j if j < H else j - H, :])
                if j < len(steps):
                    steps[j]()
            dve.wait_ge(g_cols, 2)
            dve.wait_ge(rows_out, 32)
            dve.wait_ge(smp_in, 32)

            def head(h, i):
                def o_(j):
                    return i.times(PAN) + (O_MIX + j)

                def u_(j):
                    return i.times(2 * PAN) + (U_MIX + 2 * j)

                def col(t, n):
                    return t[:, bass.ds(h + n, 1)]

                splits(u_(0))
                evac(o_(0), u_(0) + 1, qkv[:, 0, :])
                splits(u_(1))
                summed(u_(1) + 1)
                stt(halves(qkv[:, 1, :]), out_view(o_(1)), SCALE, halves(rstd[:, :]), ALU.mult, ALU.mult)\
                    .then_inc(evacuated, 1)
                splits(u_(2))
                evac(o_(2), u_(2) + 1, qkv[:, 2, :])
                dve.wait_ge(evacuated, (o_(2) + 1).value())
                dve.wait_ge(rows_in, (i + 1).times(16).value())
                link(tt(q_in[:, :], qkv[:, 0, :], rows[:, 1, :], ALU.mult))
                tt(by_smp(nq[:, :]), by_smp(q_in[:, SEQ:T]),
                   n_smp[:, h, :].unsqueeze(2).broadcast_to([P, NB, NT]), ALU.mult)
                for c in range(CH):
                    ts(dmat[:, c, :], rows[:, 0, P * c:P * c + P], cols[:, 0, c, bass.ds(h, 1)], 0.0, ALU.add, ALU.min)
                ts(dmat_s[:, :], rows[0:NS, 0, SEQ:T], cols[0:NS, 0, CH, bass.ds(h, 1)], 0.0, ALU.add, ALU.min)\
                    .then_inc(clamped, 1)
                splits(u_(3))
                evac(o_(3), u_(3) + 1, va_t[:, :])
                splits(u_(4))
                dve.wait_ge(tok_tr, (i + 1).value())
                copy(v_tok[:, 0:CH, :].rearrange("p c d -> p (c d)"), b5)
                dve.wait_ge(decayed, (i + 1).times(2).value())
                link(tt(dmat[:, :, :].rearrange("p c t -> p (c t)"), b7, dmat[:, :, :].rearrange("p c t -> p (c t)"),
                        ALU.mult))
                tt(dmat[:, :, :], dmat[:, :, :], cst[:, C_TRI:C_TRI + P].unsqueeze(1).broadcast_to([P, CH, P]), ALU.mult)
                dve.wait_ge(k_copied, (i + 1).times(CH + 1).value())
                copy(v_tok[0:NS, CH, :], b6[0:NS, P:2 * P])
                link(tt(dmat_s[:, :], b6[0:NS, 2 * P:2 * P + NS], dmat_s[:, :], ALU.mult))
                tt(dmat_s[:, :], dmat_s[:, :], cst[0:NS, C_STRI:C_STRI + NS], ALU.mult)
                for k in range(2):
                    blk = cst[0:NS, C_BLK + 4 * k:C_BLK + 4 * k + 4]
                    m = tt(vws[k][0:NS, :].rearrange("p (b d) -> p b d", d=P),
                           v_tok[0:NS, CH, :].unsqueeze(1).broadcast_to([NS, 4, P]),
                           blk.unsqueeze(2).broadcast_to([NS, 4, P]), ALU.mult)
                m.then_inc(prods, 1)
                link(nc.vector.memset(pe1[:, 0:PST], 0.0))
                evac_ext(o_(4), u_(4) + 1, pe1, PST)
                dve.wait_ge(ext_in, (i + 1).times(16).value())
                fac = [cst[:, bass.ds(h * 4 + (C_PF + k), 1)] for k in range(4)]
                y_b = y_t[:, H + h, :]
                t_p, t_s = qkv[:, 1, 0:PST + SEQ], rows[:, 0, 0:NB * (PST + NT)].rearrange("p (b t) -> p b t", b=NB)
                e_p, e_s = pe2[:, 0:PST + SEQ], smp(pe2, PST)
                link(stt(pe2[:, 1:PEXT], pe1[:, 0:PEXT - 1], fac[0], pe1[:, 1:PEXT], ALU.mult, ALU.add))
                stt(t_p[:, 3:], e_p[:, 1:PST + SEQ - 2], fac[1], e_p[:, 3:], ALU.mult, ALU.add)
                link(stt(t_s[:, :, 3:], e_s[:, :, 1:PST + NT - 2], fac[1], e_s[:, :, 3:], ALU.mult, ALU.add))
                stt(e_p[:, 7:], t_p[:, 3:PST + SEQ - 4], fac[2], t_p[:, 7:], ALU.mult, ALU.add)
                link(stt(e_s[:, :, 7:], t_s[:, :, 3:PST + NT - 4], fac[2], t_s[:, :, 7:], ALU.mult, ALU.add))
                stt(y_b[:, 0:SEQ], e_p[:, 7:PST + SEQ - 8], fac[3], e_p[:, PST:], ALU.mult, ALU.add)
                link(stt(by_smp(y_b[:, SEQ:T]), e_s[:, :, 7:PST + NT - 8], fac[3], e_s[:, :, PST:], ALU.mult, ALU.add))
                inv = cst[:, bass.ds(h * (PST + 1) + C_INV, PST)]
                link(tt(y_b[:, 0:PST], y_b[:, 0:PST], inv, ALU.mult))
                tt(y_b[:, 0:PST], y_b[:, 0:PST], pe1[:, PST:2 * PST], ALU.subtract)
                stt(y_b[:, PST:SEQ], y_b[:, PST:SEQ], col(cst, C_PW), pe1[:, 2 * PST:PST + SEQ], ALU.mult, ALU.subtract)
                stt(by_smp(y_b[:, SEQ:T]), by_smp(y_b[:, SEQ:T]), col(cst, C_PW), smp(pe1, PST)[:, :, PST:],
                    ALU.mult, ALU.subtract).then_inc(pooled, 1)
                splits(u_(5))
                dve.wait_ge(updates, (i + 1).value())
                copy(state[:, 0, 0:P], b4[:, 0:P])
                link(copy(state[:, 0, P:P + 1], b7[:, 0:1]))
                for c in range(1, CH):
                    dec = rows[:, 1, P * c + P - 1:P * c + P]
                    stt(state[:, c, 0:P], state[:, c - 1, 0:P], dec, b4[:, P * c:P * c + P], ALU.mult, ALU.add)
                    link(stt(state[:, c, P:P + 1], state[:, c - 1, P:P + 1], dec, b7[:, c:c + 1], ALU.mult, ALU.add))
                for b in range(NB // 2):
                    dec = rows[:, 1, SEQ + NT * b + NT - 1:SEQ + NT * b + NT]
                    stt(c_smp[:, b, :], c_smp[:, b, :], dec, b6[:, P * b:P * b + P], ALU.mult, ALU.add)
                n_new = n_smp[:, h, :]
                link(tt(n_new, n_new, by_smp(rows[:, 1, SEQ:T])[:, :, NT - 1], ALU.mult))
                tt(n_new, b7[:, CH:CH + NB], n_new, ALU.add)
                copy(den_t[:, 0:P], dmat[:, 0, :])
                for c in range(1, CH):
                    m = stt(den_t[:, P * c:P * c + P], q_in[:, P * c:P * c + P], state[:, c - 1, P:P + 1], dmat[:, c, :],
                            ALU.mult, ALU.add)
                m.then_inc(chained, 1)
                y_d = y_t[:, 3 * H + h, :]
                evac(o_(5), u_(5) + 1, y_d)
                splits(u_(6))
                dve.wait_ge(sums, (i + 1).value())
                stt(q_in[:, 0:SEQ], b7, -1.0, rows[:, 2, 0:SEQ], ALU.mult, ALU.max)
                link(stt(q_in[:, SEQ:T], b5[:, 64:64 + NS], -1.0, rows[:, 2, SEQ:T], ALU.mult, ALU.max))
                tt(q_in[:, 0:SEQ], b7, q_in[:, 0:SEQ], ALU.max)
                link(tt(q_in[:, SEQ:T], b5[:, 64:64 + NS], q_in[:, SEQ:T], ALU.max))
                link(nc.vector.reciprocal(q_in[:, :], q_in[:, :]))
                tt(h_t[:, 0:SEQ], b4, q_in[:, 0:SEQ], ALU.mult)
                tt(h_t[:, SEQ:T], b5[:, 0:NS], q_in[:, SEQ:T], ALU.mult).then_inc(h_ready, 1)
                for b in range(NB // 2, NB):
                    dec = rows[:, 1, SEQ + NT * b + NT - 1:SEQ + NT * b + NT]
                    m = stt(c_smp[:, b, :], c_smp[:, b, :], dec, b6[:, P * (b - 4):P * (b - 4) + P], ALU.mult, ALU.add)
                m.then_inc(chained, 1)
                dve.wait_ge(conv_in, (i + 1).times(16).value())
                link(nc.vector.memset(dx_e[:, 0:2], 0.0))
                evac_ext(o_(6), u_(6) + 1, dx_e, 2)
                tt(dx_e[:, 2:2 + SEQ], dx_e[:, 2:2 + SEQ], y_d[:, 0:SEQ], ALU.mult)
                link(tt(smp(dx_e, 2)[:, :, 2:], smp(dx_e, 2)[:, :, 2:], by_smp(y_d[:, SEQ:T]), ALU.mult))
                link(conv3(dcv, dx_e, lambda k: vec[:, bass.ds(h * 3 + (V_DC + k), 1)]))
                splits(u_(7))
                evac(o_(7), u_(7) + 1, y_d)
                dve.wait_ge(evacuated, (o_(7) + 1).value())
                tt(y_d[:, 0:SEQ], y_d[:, 0:SEQ], dcv[:, 0:SEQ], ALU.mult)
                tt(by_smp(y_d[:, SEQ:T]), by_smp(y_d[:, SEQ:T]), smp(dcv, 2)[:, :, 0:NT], ALU.mult).then_inc(d_done, 1)
                y_c = y_t[:, 2 * H + h, :]
                dve.wait_ge(h_root, (i + 1).times(2).value())
                link(nc.vector.reciprocal(q_in[:, :], q_in[:, :]))
                link(tt(h_t, h_t, q_in[:, :], ALU.mult))
                stt(y_c, h_t, col(vec, V_MN), y_c, ALU.mult, ALU.mult).then_inc(c_done, 1)
                dve.wait_ge(mixed, (i + 1).value())
                dve.wait_ge(a_in, (i + 1).times(48).value())
                y_a = y_t[:, h, :]
                tt(va_t[:, 0:SEQ], b4, bs_t[:, 0:SEQ], ALU.add)
                link(tt(h_tmp[:, :], b5[:, 0:NS], bs_t[:, SEQ:T], ALU.add))
                tt(y_a[:, 0:SEQ], va_t[:, 0:SEQ], y_a[:, 0:SEQ], ALU.mult)
                tt(y_a[:, SEQ:T], h_tmp[:, :], y_a[:, SEQ:T], ALU.mult).then_inc(a_done, 1)
                ts(halves(y_b), ps_b[:, :, 0:TH], col(vec, V_PS), None, ALU.mult).then_inc(b_done, 1)

            dve.wait_ge(u_act, H)
            dve.wait_ge(o_gate, H)
            LINKS = 25
            with dve.Fori(0, H) as h:
                link.enter(h, LINKS)
                head(h, Index(0, h, 1))
            link.leave(H)
            dve.wait_ge(c_done, H)
            dve.wait_ge(b_done, H)
            act_chunks(U_OUT, K_Y, y_t)
            for m in range(KD):
                if m:
                    splits(Index(U_OUT + 2 * m))
                if m % 4 == 0:
                    dve.wait_ge(x_back[m // 4], 16)
                summed(Index(U_OUT + 2 * m + 1))
                add_to_x(Index(O_OUT + m), m)
            act_chunks(U_Q, K_CROSS, x_t, V_CROSS)
            inv_root(S_CROSS, rstd[:, :])
            for m in range(H):
                if m:
                    splits(Index(U_Q + 2 * m))
                evac(Index(O_Q + m), Index(U_Q + 2 * m + 1), q_t[:, m, :])
            dve.wait_ge(pad_zero, 1)
            dve.wait_ge(evacuated, O_Q + H)
            for b in range(NB):
                m = copy(q_pad[:, :, b, NT * b:NT * b + NT], q_t[:, :, SEQ + NT * b:SEQ + NT * b + NT])
            m.then_inc(pad_ready, 1)
            for i in range(CH + 1):
                r = P if i < CH else NS
                dve.wait_ge(scored, i + 1)
                link(nc.vector.tensor_reduce(top[0:r, :], ps_a[0:r, :, :].rearrange("p a (h m) -> p (a h) m", m=NM),
                                             AX.X, ALU.max))
                ts(neg_top[0:r, :], top[0:r, :], -SCALE, None, ALU.mult).then_inc(topped, 1)
                dve.wait_ge(exped, H * (i + 1))
                link(nc.vector.reciprocal(p_inv[0:r, :], p_sum[0:r, :]))
                tt(prob[0:r, :, :], prob[0:r, :, :], p_inv[0:r, :].unsqueeze(2).broadcast_to([r, H, NM]), ALU.mult)\
                    .then_inc(normed, 1)
                dve.wait_ge(turned, i + 1)
                copy(prob_t[:, 4:8, 0:r], b7.rearrange("p (n t) -> p n t", n=4)[:, :, 0:r]).then_inc(turn_v, 1)
                dve.wait_ge(o_hi_done, i + 1)
                tt(o_lo[:, :, P * i:P * i + r], b4.rearrange("p (n t) -> p n t", n=4)[:, :, 0:r],
                   o_hi[:, :, P * i:P * i + r], ALU.subtract).then_inc(o_lo_done, 1)
            for m in range(KD):
                if m % 2 == 0:
                    splits(Index(U_O + m // 2), 1)
                dve.wait_ge(half_used, 2 * U_O + m + 1)
                add_to_x(Index(O_O + m), m)
            act_chunks(U_FFN, K_FFN, x_t, V_FFN)
            inv_root(S_FFN, rstd[:, :])
            dve.wait_ge(fs_in, 32)
            for e in ext:
                link(nc.vector.memset(e[:, 0:2], 0.0))

            def hidden(u0, o0, j, c, first):
                for k in range(2):
                    n = (c.times(2) + k).value()
                    if not (first and j == 0 and k == 0):
                        splits(u0 + (4 * j + 2 * k))
                    ts(smp(ext[k], 2)[:, :, 0:2], f_state[:, n, 0:2 * NB].rearrange("p (b t) -> p b t", t=2), 1.0, None,
                       ALU.mult)
                    evac_ext(o0 + (2 * j + k), u0 + (4 * j + 2 * k + 1), ext[k], 2)
                    m = conv3(cv[k], ext[k], lambda t: f_taps[:, n, t:t + 1])
                    if k == 0:
                        m.then_inc(g_conv, 1)
                    else:
                        link(m)
                    ts(f_state[:, n, 0:2 * NB].rearrange("p (b t) -> p b t", t=2), smp(ext[k], 2)[:, :, NT:NT + 2], 1.0, None,
                       ALU.mult)
                    link(ts(f_state[:, n, 2 * NB:2 * NB + 2], ext[k][:, SEQ:SEQ + 2], 1.0, None, ALU.mult))
                dve.wait_ge(g_silu, (c + 1).value())
                tt(cv[0][:, 0:CEXT - 2], cv[0][:, 0:CEXT - 2], cv[1][:, 0:CEXT - 2], ALU.mult).then_inc(h_prod, 1)
                dve.wait_ge(h_hi_done, (c + 1).times(2).value())
                tt(h_lo[:, j, 0:SEQ], cv[0][:, 0:SEQ], h_hi[:, j, 0:SEQ], ALU.subtract).then_inc(h_lo_done, 1)
                tt(by_smp(h_lo[:, j, SEQ:T]), smp(cv[0], 2)[:, :, 0:NT], by_smp(h_hi[:, j, SEQ:T]), ALU.subtract)\
                    .then_inc(h_lo_done, 1)

            def group(u0, o0, c0, first=False):
                for j in range(GRP):
                    hidden(u0, o0, j, c0 + j, first)
                for m in range(KD):
                    splits(u0 + (4 * GRP + m), 1)
                    summed(u0 + (4 * GRP + m))
                    add_to_x(o0 + (2 * GRP + m), m)

            group(Index(U_FFN), Index(O_FFN), Index(0), first=True)
            with dve.Fori(1, NG) as g:
                link.enter(g, GRP * 7, 1)
                group(Index(U_FFN, g, FU), Index(O_FFN, g, FO), Index(0, g, GRP))
            link.leave(NG - 1, 1)
            for j in range(REST):
                hidden(Index(U_LAST), Index(O_LAST), j, Index(NG * GRP + j), False)
            for m in range(KD):
                if m % 2 == 0:
                    splits(Index(U_LDN + m // 2), 1)
                dve.wait_ge(half_used, 2 * U_LDN + m + 1)
                add_to_x(Index(O_LDN + m), m)
            inv_root(S_FIN, rstd[:, :])
            for k in range(KD):
                stt(x_t[:, k, :], x_t[:, k, :], vec[:, V_FIN + k:V_FIN + k + 1], rstd[:, :], ALU.mult, ALU.mult)\
                    .then_inc(y_done, 1)


def weight_units(i):
    def cols(w, a):
        return w[:, a:a + P]

    def panel(w):
        k = w.shape[0] // P
        return w.reshape(k // UB, UB, P, P).transpose(0, 2, 1, 3).reshape(k // UB, P, UB * P)

    w_in, w_up, w_down, w_o = i["w_in"][0], i["w_up"][0], i["w_down"][0], i["w_o"][0]
    out = np.zeros((N_UNITS, P, UB * P), np.float32)
    at = 0

    def put(units):
        nonlocal at
        out[at:at + units.shape[0], :, 0:units.shape[2]] = units
        at += units.shape[0]

    for n in range(8):
        put(panel(cols(i["w_kv"][0], P * n)))
    gates = np.zeros((D, P), np.float32)
    gates[:, 0:H] = w_in[:, 10 * GW:10 * GW + H]
    gates[:, 32:32 + H] = w_in[:, 10 * GW + H:10 * GW + 2 * H]
    put(panel(gates))
    for part in (6, 0):
        for h in range(H):
            put(panel(cols(w_in, part * GW + P * h)))
    for h in range(H):
        for part in (3, 4, 5, 1, 2, 8, 9, 7):
            put(panel(cols(w_in, part * GW + P * h)))
    for m in range(KD):
        put(panel(cols(i["w_out"][0], P * m)))
    for m in range(H):
        put(panel(cols(i["w_q"][0], P * m)))
    for m in range(0, KD, 2):
        put(panel(np.concatenate([cols(w_o, P * m), cols(w_o, P * m + P)])))
    for c0 in range(0, JF, GRP):
        n = min(GRP, JF - c0)
        for c in range(c0, c0 + n):
            put(panel(cols(w_up, P * c)))
            put(panel(cols(w_up, DFF + P * c)))
        rows = w_down[P * c0:P * (c0 + n)]
        if n == GRP:
            for m in range(KD):
                put(panel(cols(rows, P * m)))
        else:
            for m in range(0, KD, 2):
                two = np.concatenate([cols(rows, P * m), cols(rows, P * m + P)])
                put(two.reshape(1, 2 * n, P, P).transpose(0, 2, 1, 3).reshape(1, P, 2 * n * P))
    assert at == N_UNITS
    return out


def constants():
    c = np.zeros((P, N_CST), np.float32)
    c[:, C_ID:C_ID + P] = np.eye(P)
    c[:, C_ONE:C_ONE + P] = 1
    c[:, C_TRI:C_TRI + P] = np.triu(np.ones((P, P)))
    for b in range(NB):
        s = slice(NT * b, NT * b + NT)
        c[s, C_STRI + NT * b:C_STRI + NT * b + NT] = np.triu(np.ones((NT, NT)))
        c[s, C_BLK + b] = 1
    for h in range(H):
        w = 2 ** (h + 1)
        for k in range(4):
            c[:, C_PF + 4 * h + k] = float(k <= h)
        c[:, C_PW + h] = 1.0 / w
        for t in range(PST + 1):
            c[:, C_INV + (PST + 1) * h + t] = 1.0 / min(t + 1, w)
    c[:, C_EPS] = EPS
    return c


def by_feature(v):
    v = v.reshape(v.shape[:-1] + (v.shape[-1] // P, P))
    return np.ascontiguousarray(np.moveaxis(np.moveaxis(v, -1, 0), -1, 1))


def vectors(i):
    v = np.zeros((P, N_VEC), np.float32)
    for at, name in ((V_MEM, "mem_norm"), (V_MIX, "norm_mix"), (V_CROSS, "norm_cross"), (V_FFN, "norm_ffn")):
        v[:, at:at + KD] = by_feature(i[name][0])
    v[:, V_FIN:V_FIN + KD] = by_feature(i["final_norm"])
    v[0:H, V_BG] = i["b_gate"][0, 0:H]
    v[32:32 + H, V_BG] = i["b_gate"][0, H:2 * H]
    v[:, V_PS:V_PS + H] = by_feature(i["pool_scale"][0])
    v[:, V_MN:V_MN + H] = by_feature(i["mlstm_norm"][0])
    v[:, V_DC:V_DC + 3 * H] = by_feature(i["w_dconv"][0]).reshape(P, 3 * H)
    return v


def laid_out(i):
    f = np.float32
    x = np.concatenate([i["x_prompt"][0], i["x_sample"].reshape(NS, D)])
    w_s, b_s = i["w_s"][0], i["b_s"][0]
    w_s_smp = np.zeros((H, NS, NS), f)
    for b in range(NB):
        s = slice(NT * b, NT * b + NT)
        w_s_smp[:, s, s] = w_s[:, 0:NT, 0:NT].transpose(0, 2, 1)
    kc = i["cache_mem_k"][0].transpose(3, 2, 0, 1)
    vc = i["cache_mem_v"][0].reshape(NB, MT, P, GW).transpose(2, 0, 1, 3)
    up = i["state_ffn_conv"][0]
    pair = by_feature(up).reshape(P, 2, JF, NB, 2).transpose(0, 2, 1, 3, 4).reshape(P, 2 * JF, 2 * NB)
    taps = by_feature(i["w_fconv"][0]).reshape(P, 2, JF, 3).transpose(0, 2, 1, 3).reshape(P, 2 * JF, 3)
    heads = lambda a: a.reshape(NB, -1, H, P).transpose(2, 3, 0, 1)
    return {
        "wall": weight_units(i),
        "x": by_feature(x),
        "mem": by_feature(i["mem_prompt"][0]),
        "cst": constants(),
        "vec": vectors(i),
        "m_smp": i["state_mlstm_m"][0].T,
        "n_smp": i["state_mlstm_n"][0].transpose(2, 1, 0),
        "c_smp": i["state_mlstm_c"][0].transpose(1, 3, 0, 2),
        "b_s": np.concatenate([np.tile(b_s, (1, CH)), np.tile(b_s[:, 0:NT], (1, NB))], axis=1),
        "w_s": w_s.transpose(0, 2, 1),
        "w_s_smp": w_s_smp,
        "w_pool": i["w_pool"][0],
        "pool_st": heads(i["state_pool"][0]),
        "conv_st": heads(i["state_conv"][0]),
        "k_cache": kc,
        "v_cache": vc,
        "ffn_st": pair,
        "w_fconv": taps,
    }


OUTPUTS = {
    "y": (P, KD, T), "mem_k": (P, H, NM), "mem_v": (P, MT, GW), "m_all": (H, T),
    "c_p": (H, P, P + 1), "c_s": (H, P, NB, P), "n_s": (H, P, NB), "v_rows": (H, P, NS),
    "pool_p": (H, P, PST), "pool_s": (H, P, NB, PST), "conv_p": (H, P, 2), "conv_s": (H, P, NB, 2),
    "ffn_st": (P, 2 * JF, 2 * NB + 2),
}


def kernel(**inputs):
    import concourse.bacc as bacc
    from concourse.bass_utils import run_bass_kernel_spmd

    i = {k: np.asarray(v) for k, v in inputs.items()}
    arrays, ins, outs = {}, {}, {}
    nc = bacc.Bacc("TRN2", target_bir_lowering=False, num_devices=1)
    for name, a in laid_out(i).items():
        arrays["in_" + name] = a = np.ascontiguousarray(a)
        ins[name] = nc.dram_tensor("in_" + name, a.shape, mybir.dt.from_np(a.dtype), kind="ExternalInput").ap()
    for name, shape in OUTPUTS.items():
        outs[name] = nc.dram_tensor("out_" + name, shape, F32, kind="ExternalOutput").ap()
    build(nc, ins, outs)
    r = run_bass_kernel_spmd(nc, [arrays], core_ids=[0]).results[0]
    o = {name: np.asarray(r["out_" + name]) for name in OUTPUTS}

    y = o["y"].transpose(2, 1, 0).reshape(T, D)
    per_head = lambda a: a.transpose(*range(2, a.ndim), 0, 1).reshape(a.shape[2:] + (GW,))
    ffn = o["ffn_st"].reshape(P, JF, 2, 2 * NB + 2).transpose(3, 2, 1, 0).reshape(2 * NB + 2, 2 * DFF)
    c_p, m_all = o["c_p"], o["m_all"]
    out = (
        y[None, 0:SEQ], y[SEQ:].reshape(NB, NT, D),
        per_head(o["pool_p"])[None, None], per_head(o["conv_p"])[None, None],
        c_p[:, :, 0:P].transpose(0, 2, 1)[None, None], c_p[:, :, P][None, None], m_all[:, SEQ - 1][None, None],
        ffn[2 * NB:][None, None],
        o["mem_k"].transpose(2, 1, 0)[None, None], o["mem_v"].transpose(1, 0, 2).reshape(NM, H, P)[None, None],
        per_head(o["v_rows"]).reshape(1, NB, NT, GW), per_head(o["pool_s"])[None], per_head(o["conv_s"])[None],
        o["c_s"].transpose(2, 0, 3, 1)[None], o["n_s"].transpose(2, 0, 1)[None],
        m_all[:, SEQ:].reshape(H, NB, NT)[:, :, NT - 1].T[None], ffn[0:2 * NB].reshape(1, NB, 2, 2 * DFF),
    )
    return tuple(np.ascontiguousarray(a) for a in out)
```

```python
from contextlib import ExitStack

import numpy as np

import concourse.bass as bass
from concourse import mybir

F32 = mybir.dt.float32
F32R = mybir.dt.float32r
ALU = mybir.AluOpType
ACT = mybir.ActivationFunctionType
AX = mybir.AxisListType

P = 128
D = 2048
KD = D // P
SEQ = 512
NB, NT = 8, 4
NS = NB * NT
T = SEQ + NS
TH = T // 2
H = 4
GW = H * P
NM = 256
MT = NM // P
DFF = 5504
JF = DFF // P
CH = SEQ // P
PST = 15
EPS = 1e-6
SCALE = float(P) ** -0.5

UB = 8
RING = 4
GRP = 8
NG = JF // GRP
REST = JF - NG * GRP

U_MEM, O_MEM = 0, 0
U_GATE, O_GATE = U_MEM + 2 * 8, O_MEM + 8
U_PRE, O_PRE = U_GATE + 2, O_GATE + 1
U_MIX, O_MIX = U_PRE + 2 * 2 * H, O_PRE + 2 * H
MIXERS = "CDAB"
FREE_LO = KD - 2 * H
PAN = 8
U_OUT, O_OUT = U_MIX + 2 * PAN * H, O_MIX + PAN * H
U_Q, O_Q = U_OUT + 2 * KD, O_OUT + KD
U_O, O_O = U_Q + 2 * H, O_Q + H
U_FFN, O_FFN = U_O + KD // 2, O_O + KD
FU, FO = 2 * 2 * GRP + KD, 2 * GRP + KD
U_LAST, O_LAST = U_FFN + NG * FU, O_FFN + NG * FO
U_LDN, O_LDN = U_LAST + 4 * REST, O_LAST + 2 * REST
LDN_UNITS = KD // 2
N_UNITS = U_LDN + LDN_UNITS
Y_PARTS = [[(k, k + 4) for k in range(0, KD, 4)], [(0, 2), (2, 6), (6, 10), (10, 14), (14, 16)]]
ROOT_AT, NORM_AT = 1, 3
WARM_FIRST, WARM_LAST = 9, 12

C_ID, C_ONE, C_TRI = 0, P, 2 * P
C_STRI = 3 * P
C_BLK = C_STRI + NS
C_PF = C_BLK + NB
C_PW = C_PF + 4 * H
C_INV = C_PW + H
C_EPS = C_INV + (PST + 1) * H
N_CST = C_EPS + 2
V_MEM, V_MIX, V_CROSS, V_FFN, V_FIN = [KD * n for n in range(5)]
V_BG = 5 * KD
V_PS = V_BG + 1
V_MN = V_PS + H
V_DC = V_MN + H
N_VEC = V_DC + 3 * H

EP = PST + SEQ
ES = PST + NT
PEXT = EP + NB * ES
CP = 2 + SEQ
CS = 2 + NT
CEXT = CP + NB * CS
CV = CEXT - 2


class Index:

    def __init__(self, const, reg=None, step=0):
        self.const, self.reg, self.step = const, reg, step

    def __add__(self, k):
        return Index(self.const + k, self.reg, self.step)

    def __sub__(self, k):
        return self + (-k)

    def value(self):
        return self.const if self.reg is None else self.reg * self.step + self.const

    def mod(self, m):
        assert self.step % m == 0
        return self.const % m

    def over(self, m):
        assert self.step % m == 0
        return Index(self.const // m, self.reg, self.step // m)

    def times(self, m):
        return Index(self.const * m, self.reg, self.step * m)


class Chain:

    def __init__(self, eng, sem):
        self.eng, self.sem, self.at = eng, sem, Index(0)

    def __call__(self, ins):
        ins.then_inc(self.sem, 1)
        self.at = self.at + 1
        self.eng.wait_ge(self.sem, self.at.value())

    def enter(self, reg, per, first=0):
        self.start, self.per = self.at.const, per
        self.at = Index(self.at.const - first * per, reg, per)

    def leave(self, times, first=0):
        used = self.at.const - (self.start - first * self.per)
        assert used == self.per, f"links in a round: {used}, not {self.per}"
        self.at = Index(self.start + times * self.per)


class Place:

    def __init__(self, at, spans):
        self.at, self.spans = at, [list(s) for s in spans]

    def take(self, name, shape, dt=F32):
        n = -(-int(np.prod(shape[1:])) * 4 // 32) * 32
        for s in self.spans:
            if s[1] - s[0] >= n:
                s[0] += n
                return self.at(name, s[0] - n, shape, dt)
        raise ValueError(f"no room for {name}")


def build(nc, ins, outs):
    ctx = ExitStack()
    with ctx:
        def sem(name):
            return ctx.enter_context(nc.semaphore(name))

        base = -(-nc.sbuf_base // 64) * 64

        def at(name, offset, shape, dt=F32):
            return nc.alloc_sbuf_tensor_at(name, shape, dt, offset=base + offset)

        ACT_B, UNIT_B = KD * T * 4, UB * P * 4
        R_X = 0
        R_AH = R_X + ACT_B
        R_AL = R_AH + ACT_B
        R_Y = R_AL + ACT_B
        R_RAW = R_Y + ACT_B
        R_WH = R_RAW + RING * UNIT_B
        R_WL = R_WH + RING * UNIT_B
        R_CST = R_WL + RING * UNIT_B
        R_VEC = R_CST + -(-N_CST * 4 // 32) * 32
        R_RSTD = R_VEC + -(-N_VEC * 4 // 32) * 32
        R_SQA = R_RSTD + T * 4
        R_MKV = R_SQA + T * 4
        R_FREE = R_MKV + 2 * H * NM * 4
        R_END = (nc.sbuf_usable_end - base) // 32 * 32
        R_SQT = R_END - 2 * T * 4

        x_t = at("x_t", R_X, [P, KD, T])
        a_hi = at("a_hi", R_AH, [P, KD, T], F32R)
        a_lo = at("a_lo", R_AL, [P, KD, T], F32R)
        m_raw = at("m_raw", R_AL, [P, KD, NM])
        y_t = at("y_t", R_Y, [P, KD, T])
        m_hi = at("m_hi", R_Y, [P, KD, NM], F32R)
        m_lo = at("m_lo", R_Y + KD * NM * 4, [P, KD, NM], F32R)
        kc_t = at("kc_t", R_Y, [P, H, NB, NM])
        h_hi = at("h_hi", R_Y, [P, GRP, T], F32R)
        h_lo = at("h_lo", R_Y + GRP * T * 4, [P, GRP, T], F32R)
        l_hi = at("l_hi", R_AH, [P, LDN_UNITS - RING, UB * P], F32R)
        l_lo = at("l_lo", R_AL, [P, LDN_UNITS - RING, UB * P], F32R)
        w_raw = at("w_raw", R_RAW, [P, RING, UB * P])
        w_hi = at("w_hi", R_WH, [P, RING, UB * P], F32R)
        w_lo = at("w_lo", R_WL, [P, RING, UB * P], F32R)
        cst = at("cst", R_CST, [P, N_CST])
        vec = at("vec", R_VEC, [P, N_VEC])
        rstd = at("rstd", R_RSTD, [P, T])
        sq_sum = at("sq_sum", R_SQA, [P, T])
        mk_t = at("mk_t", R_MKV, [P, H, NM])
        mv_t = at("mv_t", R_MKV + H * NM * 4, [P, MT, GW])
        sq_tmp = at("sq_tmp", R_SQT, [P, 2, T])
        vt_mem = at("vt_mem", R_FREE, [P, H, NM])
        rstd_m = rstd[:, 0:NM]
        assert R_FREE + H * NM * 4 <= R_SQT

        mix = Place(at, [(R_X, R_AH), (R_FREE, R_END)])
        qkv = mix.take("qkv", [P, 3, T])
        rows = mix.take("rows", [P, 3, T])
        q_in = mix.take("q_in", [P, T])
        k_tok = mix.take("k_tok", [P, CH + 1, P])
        v_tok = mix.take("v_tok", [P, CH + 1, P])
        dmat = mix.take("dmat", [P, CH, P])
        dmat_s = mix.take("dmat_s", [NS, NS])
        state = mix.take("state", [P, CH, P + 1])
        c_smp = mix.take("c_smp", [P, NB, P])
        n_smp = mix.take("n_smp", [P, H, NB])
        cols = mix.take("cols", [P, 2, CH + 1, H])
        nq = mix.take("nq", [P, NS])
        h_tmp = mix.take("h_tmp", [P, NS])
        va_t = mix.take("va_t", [P, T])
        va_tok = mix.take("va_tok", [P, CH + 1, P])
        bs_t = mix.take("bs_t", [P, T])
        ws_t = mix.take("ws_t", [P, P])
        wd_t = mix.take("wd_t", [NS, NS])
        wp_t = mix.take("wp_t", [P, P])
        pe1 = mix.take("pe1", [P, PEXT])
        pe2 = mix.take("pe2", [P, PEXT])
        dx_e, dcv = pe1[:, 0:CEXT], pe2[:, 0:CEXT]
        den_t, h_t = qkv[:, 1, 0:SEQ], qkv[:, 1, :]
        vws = [qkv[:, 2, 0:4 * P], qkv[:, 0, 0:4 * P]]

        gt = Place(at, [(R_X + 3 * T * 4, R_AH)])
        gate = gt.take("gate", [P, T])
        scan_p = [gt.take(f"scan_p{n}", [H, CH, P // 2 + P]) for n in range(2)]
        scan_s = [gt.take(f"scan_s{n}", [H, NB, 2 + NT]) for n in range(2)]
        f_row = gt.take("f_row", [H, T])
        b_row = gt.take("b_row", [H, T])
        a_row = gt.take("a_row", [H, T])
        m_row = gt.take("m_row", [H, T])
        w_row = gt.take("w_row", [H, T])
        r3 = gt.take("r3", [H, 3, T])
        m_prev = gt.take("m_prev", [H, CH])
        ms_in = gt.take("ms_in", [H, NB])

        q_t = at("q_t", R_FREE, [P, H, T])
        assert R_FREE + H * T * 4 <= R_END
        vc_t = at("vc_t", R_AH, [P, NB, MT, GW])
        assert NB * MT * GW * 4 + 2 * NB * NS * 4 <= ACT_B and MT * GW == H * NM
        R_O = R_AL + FREE_LO * T * 4
        o_hi = at("o_hi", R_O, [P, H, T], F32R)
        o_lo = at("o_lo", R_O + H * T * 4, [P, H, T], F32R)
        cross = Place(at, [(R_AL, R_O)])
        prob = [cross.take(f"prob{n}", [P, H, NM]) for n in range(2)]
        prob_t = [cross.take(f"prob_t{n}", [P, H * MT, P]) for n in range(2)]
        top = [cross.take(f"top{n}", [P, H]) for n in range(2)]
        neg_top = [cross.take(f"neg_top{n}", [P, H]) for n in range(2)]
        p_sum = [cross.take(f"p_sum{n}", [P, H]) for n in range(2)]
        p_inv = [cross.take(f"p_inv{n}", [P, H]) for n in range(2)]
        q_pad = [at(f"q_pad{n}", end - 2 * NB * NS * 4, [P, 2, NB, NS]) for n, end in enumerate((R_AL, R_RAW))]

        ffn = Place(at, [(R_MKV, R_END)])
        f_state = ffn.take("f_state", [P, 2 * JF, 2 * NB + 2])
        f_taps = ffn.take("f_taps", [P, 2 * JF, 3])
        ext = [ffn.take(f"ext{n}", [P, CEXT]) for n in range(2)]
        cv = [ffn.take(f"cv{n}", [P, CEXT]) for n in range(2)]

        ps_out = ctx.enter_context(nc.psum_tensor("ps_out", [P, 4, 512], F32))
        ps_a = ctx.enter_context(nc.psum_tensor("ps_a", [P, 2, 512], F32))
        ps_b = ctx.enter_context(nc.psum_tensor("ps_b", [P, 2, 512], F32))
        b4, b5, b6, b7 = ps_a[:, 0, :], ps_a[:, 1, :], ps_b[:, 0, :], ps_b[:, 1, :]
        last_q = (O_Q + H - 1) % 2
        ps_score = [ps_a, ps_out[:, 2 * (1 - last_q):2 * (1 - last_q) + 2, :]]
        ps_value = [ps_out[:, 2 * last_q + n, :].rearrange("p (h t) -> p h t", h=H) for n in range(2)]

        landed = [sem(f"landed{n}") for n in range(RING)]
        hi_ready = sem("hi_ready")
        lo_ready = sem("lo_ready")
        half_used = sem("half_used")
        evacuated = sem("evacuated")
        cst_in = sem("cst_in")
        mem_in = [sem(f"mem_in{n}") for n in range(4)]
        x_in = [sem(f"x_in{n}") for n in range(4)]
        x_back = [sem(f"x_back{n}") for n in range(4)]
        act_hi = sem("act_hi")
        act_lo = sem("act_lo")
        sq_done = sem("sq_done")
        sq_added = sem("sq_added")
        ssq = sem("ssq")
        root = sem("root")
        rstd_ready = sem("rstd_ready")
        mv_tr = sem("mv_tr")
        mv_ready = sem("mv_ready")
        f_ready = sem("f_ready")
        f_exp = sem("f_exp")
        f_exp1 = sem("f_exp1")
        f_log = sem("f_log")
        g_rows = sem("g_rows")
        g_exps = sem("g_exps")
        rows_out = sem("rows_out")
        g_tr = sem("g_tr")
        g_cols = sem("g_cols")
        smp_in = sem("smp_in")
        rows_in = sem("rows_in")
        c_in = sem("c_in")
        a_in = sem("a_in")
        ws_ready = sem("ws_ready")
        wp_in = sem("wp_in")
        ext_in = sem("ext_in")
        clamped = sem("clamped")
        decayed = sem("decayed")
        tok_tr = sem("tok_tr")
        k_copied = sem("k_copied")
        prods = sem("prods")
        updates = sem("updates")
        chained = sem("chained")
        sums = sem("sums")
        h_ready = sem("h_ready")
        h_sq = sem("h_sq")
        h_root = sem("h_root")
        o_gate = sem("o_gate")
        c_done = sem("c_done")
        c_out = sem("c_out")
        u_act = sem("u_act")
        v_act = sem("v_act")
        va_tr = sem("va_tr")
        va_copied = sem("va_copied")
        mixed = sem("mixed")
        a_done = sem("a_done")
        va_out = sem("va_out")
        pooled = sem("pooled")
        pool_out = sem("pool_out")
        b_done = sem("b_done")
        conv_in = sem("conv_in")
        conv_out = sem("conv_out")
        d_done = sem("d_done")
        kc_in = sem("kc_in")
        vc_in = sem("vc_in")
        pad_zero = sem("pad_zero")
        pad_ready = sem("pad_ready")
        scored = sem("scored")
        topped = sem("topped")
        exped = sem("exped")
        normed = sem("normed")
        turned = sem("turned")
        turn_a = sem("turn_a")
        turn_v = sem("turn_v")
        attended = sem("attended")
        o_hi_done = sem("o_hi_done")
        o_lo_done = sem("o_lo_done")
        fs_in = sem("fs_in")
        g_conv = sem("g_conv")
        g_silu = sem("g_silu")
        h_prod = sem("h_prod")
        h_hi_done = sem("h_hi_done")
        h_lo_done = sem("h_lo_done")
        y_done = sem("y_done")
        y_out = sem("y_out")
        stored = sem("stored")
        dve_order = sem("dve_order")

        wall, x_d = ins["wall"], ins["x"]
        scratch = nc.dram_tensor("gate_rows", (H, 3, T), F32, kind="Internal").ap()

        K_MEM, K_MIX, K_Y, K_CROSS, K_FFN = [KD * n for n in range(5)]
        S_MEM, S_MIX, S_CROSS, S_FFN, S_FIN = range(5)

        def y_at(mixer, h):
            return h * 4 + MIXERS.index(mixer)

        def halves(ap):
            return ap.rearrange("p (a b) -> p a b", a=2)

        def out_view(o):
            q = o.mod(2)
            return ps_out[:, 2 * q:2 * q + 2, 0:TH]

        def out_bank(o, n):
            return ps_out[:, 2 * o.mod(2) + n, :]

        def split_place(n):
            if n.reg is None and n.const >= U_LDN + RING:
                return l_hi[:, n.const - U_LDN - RING, :], l_lo[:, n.const - U_LDN - RING, :]
            return w_hi[:, n.mod(RING), :], w_lo[:, n.mod(RING), :]

        def last_bank(i):
            return ps_out[:, (2 * (O_LDN % 2) + i) % 4, 0:TH]

        def half(ap, n):
            return ap[:, n * TH:(n + 1) * TH]

        def smp(ap, before):
            return ap[:, before + SEQ:before + SEQ + NB * (before + NT)].rearrange("p (b t) -> p b t", t=before + NT)

        def by_smp(ap):
            return ap.rearrange("p (b t) -> p b t", t=NT)

        def eps(n=P):
            return cst[0:n, C_EPS:C_EPS + 1]

        block = ctx.enter_context(nc.Block())

        @block.sync
        def _(sp):
            def unit(n):
                sp.dma_start(w_raw[:, n, :], wall[n]).then_inc(landed[n], 16)

            def memory(n):
                sp.dma_start(m_raw[:, 4 * n:4 * n + 4, :], ins["mem"][:, 4 * n:4 * n + 4, :]).then_inc(mem_in[n], 16)

            unit(0)
            sp.dma_start(cst[:, :], ins["cst"]).then_inc(cst_in, 16)
            sp.dma_start(vec[:, :], ins["vec"]).then_inc(cst_in, 16)
            memory(0)
            memory(1)
            unit(1)
            memory(2)
            memory(3)
            unit(2)
            unit(3)
            for n in range(RING, 3 * RING):
                sp.wait_ge(lo_ready, n - RING + 1)
                sp.dma_start(w_raw[:, n % RING, :], wall[n]).then_inc(landed[n % RING], 16)
                if n % 2:
                    m = n // 2 - RING // 2
                    sp.dma_start(x_t[:, 4 * m:4 * m + 4, :], x_d[:, 4 * m:4 * m + 4, :]).then_inc(x_in[m], 16)
            with sp.Fori(3, N_UNITS // RING) as i:
                for j in range(RING):
                    sp.wait_ge(lo_ready, i * RING + (j - RING + 1))
                    sp.dma_start(w_raw[:, j, :], wall[i * RING + j]).then_inc(landed[j], 16)
            for n in range(N_UNITS // RING * RING, N_UNITS):
                sp.wait_ge(lo_ready, n - RING + 1)
                sp.dma_start(w_raw[:, n % RING, :], wall[n]).then_inc(landed[n % RING], 16)
            n_out = 0
            for n in range(2):
                for k, end in Y_PARTS[n]:
                    sp.wait_ge(y_done, n * KD + end)
                    sp.dma_start(outs["y"][:, k:end, n * TH:(n + 1) * TH], x_t[:, k:end, n * TH:(n + 1) * TH])\
                        .then_inc(y_out, 16)
                    n_out += 16
            sp.wait_ge(y_out, n_out)

        @block.gpsimd
        def _(pool):
            n_stored = [0]

            def store(dst, src):
                pool.dma_start(dst, src).then_inc(stored, 16)
                n_stored[0] += 16

            def squares(group, n):
                if group:
                    pool.wait_ge(ssq, group)
                for k in range(KD):
                    c = group * KD + k
                    pool.wait_ge(sq_done, c + 1)
                    if k == 0:
                        nc.gpsimd.tensor_copy(sq_sum[:, 0:n], sq_tmp[:, c % 2, 0:n]).then_inc(sq_added, 1)
                    else:
                        pool.wait_ge(sq_added, c)
                        nc.gpsimd.tensor_tensor(sq_sum[:, 0:n], sq_sum[:, 0:n], sq_tmp[:, c % 2, 0:n],
                                                ALU.add).then_inc(sq_added, 1)

            squares(S_MEM, NM)
            squares(S_MIX, T)
            pool.wait_ge(evacuated, O_MEM + H)
            store(outs["mem_k"], mk_t[:, :, :])
            pool.wait_ge(mv_ready, MT)
            store(outs["mem_v"], mv_t[:, :, :])
            pool.wait_ge(act_lo, K_Y)
            pool.wait_ge(act_hi, K_Y)
            pool.wait_ge(rstd_ready, S_MIX + 1)
            pool.dma_start(ms_in[:, :], ins["m_smp"]).then_inc(smp_in, 16)
            pool.wait_ge(g_exps, 3)
            pool.dma_start(scratch, r3[:, :, :]).then_inc(rows_out, 16)
            pool.dma_start(outs["m_all"], w_row[:, :]).then_inc(rows_out, 16)
            pool.wait_ge(rows_out, 32)
            pool.wait_ge(g_cols, 2)
            pool.dma_start(n_smp[:, :, :], ins["n_smp"]).then_inc(smp_in, 16)

            def head_loads(h, i):
                pool.dma_start(rows[:, :, :], scratch[h].partition_broadcast(P)).then_inc(rows_in, 16)
                pool.dma_start(c_smp[:, :, :], ins["c_smp"][h]).then_inc(c_in, 16)
                pool.dma_start(bs_t[:, :], ins["b_s"][h].partition_broadcast(P)).then_inc(a_in, 16)
                pool.dma_start(ws_t[:, :], ins["w_s"][h]).then_inc(a_in, 16)
                pool.dma_start(wd_t[:, :], ins["w_s_smp"][h]).then_inc(a_in, 16)
                pool.dma_start(smp(pe1, PST)[:, :, 0:PST], ins["pool_st"][h]).then_inc(ext_in, 16)
                pool.dma_start(wp_t[:, :], ins["w_pool"][h]).then_inc(wp_in, 16)
                pool.wait_ge(a_in, (i + 1).times(48).value())
                nc.gpsimd.tensor_tensor(ws_t[:, :], ws_t[:, :], cst[:, C_TRI:C_TRI + P],
                                        ALU.mult).then_inc(ws_ready, 1)
                nc.gpsimd.tensor_tensor(wd_t[:, :], wd_t[:, :], cst[0:NS, C_STRI:C_STRI + NS],
                                        ALU.mult).then_inc(ws_ready, 1)

            def head_stores(h, i):
                pool.wait_ge(v_act, (i + 1).value())
                pool.dma_start(outs["v_rows"][h], va_t[:, SEQ:T]).then_inc(va_out, 16)
                pool.wait_ge(pooled, (i + 1).value())
                pool.dma_start(outs["pool_p"][h], pe1[:, SEQ:SEQ + PST]).then_inc(pool_out, 16)
                pool.dma_start(outs["pool_s"][h], smp(pe1, PST)[:, :, NT:NT + PST]).then_inc(pool_out, 16)
                pool.wait_ge(chained, (i + 1).times(2).value())
                pool.dma_start(outs["c_p"][h], state[:, CH - 1, :]).then_inc(c_out, 16)
                pool.dma_start(outs["n_s"][h], n_smp[:, h, :]).then_inc(c_out, 16)
                pool.dma_start(outs["c_s"][h], c_smp[:, :, :]).then_inc(c_out, 16)
                pool.wait_ge(pool_out, (i + 1).times(32).value())
                pool.dma_start(smp(dx_e, 2)[:, :, 0:2], ins["conv_st"][h]).then_inc(conv_in, 16)
                pool.wait_ge(d_done, (i + 1).value())
                pool.dma_start(outs["conv_p"][h], dx_e[:, SEQ:SEQ + 2]).then_inc(conv_out, 16)
                pool.dma_start(outs["conv_s"][h], smp(dx_e, 2)[:, :, NT:NT + 2]).then_inc(conv_out, 16)
                pool.wait_ge(c_done, (i + 1).value())
                pool.wait_ge(a_done, (i + 1).value())
                pool.wait_ge(b_done, (i + 1).value())
                pool.wait_ge(c_out, (i + 1).times(48).value())
                pool.wait_ge(va_out, (i + 1).times(16).value())
                pool.wait_ge(conv_out, (i + 1).times(32).value())

            head_loads(0, Index(0))
            with pool.Fori(0, H - 1) as h:
                head_stores(h, Index(0, h, 1))
                head_loads(h + 1, Index(1, h, 1))
            head_stores(H - 1, Index(H - 1))
            for n in range(4):
                pool.dma_start(x_t[:, 4 * n:4 * n + 4, :], x_d[:, 4 * n:4 * n + 4, :]).then_inc(x_back[n], 16)
            pool.wait_ge(act_lo, K_CROSS)
            pool.wait_ge(act_hi, K_CROSS)
            pool.dma_start(kc_t[:, :, :, :], ins["k_cache"]).then_inc(kc_in, 16)
            squares(S_CROSS, T)
            pool.wait_ge(half_used, 2 * U_O)
            for pad in q_pad:
                nc.gpsimd.memset(pad[:, :, :, :], 0.0).then_inc(pad_zero, 1)
            pool.dma_start(vc_t[:, :, :, :], ins["v_cache"]).then_inc(vc_in, 16)
            pool.wait_ge(attended, CH + 1)
            pool.wait_ge(stored, 32)
            pool.dma_start(f_state[:, :, 0:2 * NB], ins["ffn_st"]).then_inc(fs_in, 16)
            pool.dma_start(f_taps[:, :, :], ins["w_fconv"]).then_inc(fs_in, 16)
            squares(S_FFN, T)
            pool.wait_ge(h_lo_done, 2 * JF)
            store(outs["ffn_st"], f_state[:, :, :])
            for n in range(2):
                for k in range(KD):
                    c = (S_FIN + n) * KD + k
                    pool.wait_ge(sq_done, c + 1)
                    if k == 0:
                        nc.gpsimd.tensor_copy(half(sq_sum, n), sq_tmp[:, c % 2, 0:TH]).then_inc(sq_added, 1)
                    else:
                        pool.wait_ge(sq_added, c)
                        nc.gpsimd.tensor_tensor(half(sq_sum, n), half(sq_sum, n), sq_tmp[:, c % 2, 0:TH],
                                                ALU.add).then_inc(sq_added, 1)
            pool.wait_ge(stored, n_stored[0])
            pool.wait_ge(rows_out, 32)
            pool.wait_ge(c_out, 48 * H)
            pool.wait_ge(va_out, 16 * H)
            pool.wait_ge(pool_out, 32 * H)
            pool.wait_ge(conv_out, 32 * H)

        @block.scalar
        def _(act):
            def split_hi(n):
                s = n.mod(RING)
                act.wait_ge(landed[s], (n.over(RING) + 1).times(16).value())
                if n.reg is None and n.const >= U_LDN + RING:
                    act.wait_ge(half_used, 2 * U_LDN)
                elif n.reg is not None or n.const >= RING:
                    act.wait_ge(half_used, (n - (RING - 1)).times(2).value())
                nc.scalar.activation(split_place(n)[0], w_raw[:, s, :], ACT.Copy).then_inc(hi_ready, 1)

            def splits(u, n=2):
                for k in range(n):
                    if u.reg is not None or u.const + 2 + k < N_UNITS:
                        split_hi(u + 2 + k)

            def square(c, src, n=T):
                if c >= 2:
                    act.wait_ge(sq_added, c - 1)
                nc.scalar.activation(sq_tmp[:, c % 2, 0:n], src, ACT.Square).then_inc(sq_done, 1)

            def rms_root(group, dst, n=T):
                act.wait_ge(ssq, group + 1)
                nc.scalar.activation(halves(dst), ps_b[:, :, 0:n // 2], ACT.Sqrt, bias=eps(),
                                     scale=1.0 / D).then_inc(root, 1)

            def act_chunks(u, src, dst, gain=None, before={}):
                for k in range(KD):
                    if k in before:
                        before[k]()
                    if k % 4 == 0:
                        act.wait_ge(half_used, 2 * (u - 2) + 1 + k // 4)
                    scale = 1.0 if gain is None else vec[:, gain + k:gain + k + 1]
                    nc.scalar.activation(dst[:, k, :], src[:, k, :], ACT.Copy, scale=scale).then_inc(act_hi, 1)
                    if k % 8 == 7:
                        split_hi(Index(u + 2 + k // 8))

            split_hi(Index(0))
            act.wait_ge(cst_in, 32)
            for k in range(KD):
                if k % 4 == 0:
                    act.wait_ge(mem_in[k // 4], 16)
                nc.scalar.activation(m_hi[:, k, :], m_raw[:, k, :], ACT.Copy,
                                     scale=vec[:, V_MEM + k:V_MEM + k + 1]).then_inc(act_hi, 1)
                square(k, m_raw[:, k, :], NM)
                if k == 7:
                    split_hi(Index(1))
            split_hi(Index(2))
            split_hi(Index(3))
            done = 0
            for o in range(1, 8):
                splits(Index(U_MEM + 2 * o))
                if o == 1:
                    rms_root(S_MEM, rstd_m, NM)
                for k in range(done, min(done + 3, KD) if o > 1 else 0):
                    if k % 4 == 0:
                        act.wait_ge(x_in[k // 4], 16)
                    nc.scalar.activation(a_hi[:, k, :], x_t[:, k, :], ACT.Copy,
                                         scale=vec[:, V_MIX + k:V_MIX + k + 1]).then_inc(act_hi, 1)
                    square(S_MIX * KD + k, x_t[:, k, :])
                    done = k + 1
            splits(Index(U_GATE))
            act.wait_ge(mv_tr, 1)
            for m in range(MT):
                nc.scalar.activation(mv_t[:, m, :], ps_a[:, m, :], ACT.Copy).then_inc(mv_ready, 1)
            rms_root(S_MIX, rstd[:, :])

            def o_or_u(j):
                act.wait_ge(evacuated, O_PRE + j + 1)
                if j < H:
                    y = y_t[:, y_at("C", j), :]
                    nc.scalar.activation(y, y, ACT.Sigmoid).then_inc(o_gate, 1)
                else:
                    y = y_t[:, y_at("A", j - H), :]
                    nc.scalar.activation(y, y, ACT.Gelu_apprx_tanh).then_inc(u_act, 1)

            splits(Index(U_PRE))
            act.wait_ge(f_ready, 1)
            nc.scalar.activation(m_row[:, :], f_row[:, :], ACT.Exp).then_inc(f_exp, 1)
            act.wait_ge(f_exp1, 1)
            nc.scalar.activation(w_row[:, :], m_row[:, :], ACT.Ln).then_inc(f_log, 1)
            for j in range(1, 5):
                splits(Index(U_PRE + 2 * j))
                o_or_u(j - 1)
            act.wait_ge(g_rows, 1)
            nc.scalar.activation(r3[:, 1, :], r3[:, 1, :], ACT.Exp, scale=-1.0).then_inc(g_exps, 1)
            nc.scalar.activation(r3[:, 2, :], w_row[:, :], ACT.Exp, scale=-1.0).then_inc(g_exps, 1)
            nc.scalar.activation(b_row[:, :], b_row[:, :], ACT.Exp).then_inc(g_exps, 1)
            for j in range(5, 8):
                splits(Index(U_PRE + 2 * j))
                o_or_u(j - 1)
            act.wait_ge(g_tr, 1)
            act.wait_ge(rows_out, 32)
            by_tok = b4[:, 0:2 * (CH + 1) * H].rearrange("p (q c h) -> p q c h", q=2, h=H)
            nc.scalar.activation(cols[:, :, 0:CH, :], by_tok[:, :, 0:CH, :], ACT.Copy).then_inc(g_cols, 1)
            nc.scalar.activation(cols[0:NS, :, CH, :], by_tok[0:NS, :, CH, :], ACT.Copy).then_inc(g_cols, 1)
            o_or_u(7)
            with act.Fori(0, H) as h:
                i = Index(0, h, 1)

                def slot(j):
                    splits(Index(U_MIX + 2 * j, h, 2 * PAN))

                slot(0)
                slot(1)
                slot(2)
                slot(3)
                act.wait_ge(clamped, (i + 1).value())
                nc.scalar.activation(dmat[:, :, :], dmat[:, :, :], ACT.Exp).then_inc(decayed, 1)
                nc.scalar.activation(dmat_s[:, :], dmat_s[:, :], ACT.Exp).then_inc(decayed, 1)
                slot(4)
                act.wait_ge(tok_tr, (i + 1).value())
                for c in range(CH):
                    nc.scalar.activation(k_tok[:, c, :], b4[:, P * c:P * c + P], ACT.Copy,
                                         scale=cols[:, 1, c, bass.ds(h, 1)]).then_inc(k_copied, 1)
                nc.scalar.activation(k_tok[0:NS, CH, :], b6[0:NS, 0:P], ACT.Copy,
                                     scale=cols[0:NS, 1, CH, bass.ds(h, 1)]).then_inc(k_copied, 1)
                act.wait_ge(evacuated, (i.times(PAN) + O_MIX + 4).value())
                nc.scalar.activation(va_t[:, :], va_t[:, :], ACT.Gelu_apprx_tanh).then_inc(v_act, 1)
                slot(5)
                slot(6)
                act.wait_ge(h_ready, (i + 1).value())
                nc.scalar.activation(q_in[:, :], h_t, ACT.Square).then_inc(h_sq, 1)
                slot(7)
                act.wait_ge(va_tr, (i + 1).value())
                nc.scalar.activation(va_tok[:, 0:CH, :].rearrange("p c d -> p (c d)"), b4, ACT.Copy).then_inc(va_copied, 1)
                nc.scalar.activation(va_tok[0:NS, CH, :], b5[0:NS, 0:P], ACT.Copy).then_inc(va_copied, 1)
                nc.scalar.activation(q_in[:, 0:SEQ], b7, ACT.Sqrt, bias=eps(), scale=1.0 / P).then_inc(h_root, 1)
                nc.scalar.activation(q_in[:, SEQ:T], b6[:, 0:NS], ACT.Sqrt, bias=eps(), scale=1.0 / P).then_inc(h_root, 1)
            act.wait_ge(b_done, H - 1)
            act_chunks(U_OUT, y_t, a_hi, before={
                y_at("C", H - 1): lambda: act.wait_ge(c_done, H),
                y_at("D", H - 1): lambda: act.wait_ge(d_done, H),
                y_at("A", H - 1): lambda: act.wait_ge(a_done, H),
                y_at("B", H - 1): lambda: act.wait_ge(b_done, H)})

            def square_x(first, group, m):
                act.wait_ge(evacuated, (m + (first + 1)).value())
                c = m + group * KD
                act.wait_ge(sq_added, (c - 1).value())
                nc.scalar.activation(sq_tmp[:, c.mod(2), :], x_t[:, m.value(), :], ACT.Square).then_inc(sq_done, 1)

            square_x(O_OUT, S_CROSS, Index(0))
            splits(Index(U_OUT + 2))
            square_x(O_OUT, S_CROSS, Index(1))
            with act.Fori(1, KD // 2 - 1) as m:
                for j in range(2):
                    splits(Index(U_OUT + 2 * j, m, 4))
                    square_x(O_OUT, S_CROSS, Index(j, m, 2))
            splits(Index(U_OUT + 2 * (KD - 2)))
            square_x(O_OUT, S_CROSS, Index(KD - 2))
            splits(Index(U_OUT + 2 * (KD - 1)))
            act_chunks(U_Q, x_t, a_hi, V_CROSS, before={12: lambda: square_x(O_OUT, S_CROSS, Index(KD - 1))})
            for m in range(1, H):
                splits(Index(U_Q + 2 * m))
                if m == 1:
                    rms_root(S_CROSS, rstd[:, :])
            def exps(i):
                r = P if i < CH else NS
                act.wait_ge(topped, i + 1)
                if i >= 2:
                    act.wait_ge(turned, i - 1)
                for h in range(H):
                    nc.scalar.activation(prob[i % 2][0:r, h, :], ps_score[i % 2][0:r, h // 2, h % 2 * NM:(h % 2 + 1) * NM],
                                         ACT.Exp, bias=neg_top[i % 2][0:r, h:h + 1], scale=SCALE,
                                         accum_out=p_sum[i % 2][0:r, h:h + 1]).then_inc(exped, 1)

            exps(0)
            exps(1)
            for i in range(CH + 1):
                r = P if i < CH else NS
                act.wait_ge(turned, i + 1)
                if i >= 2:
                    act.wait_ge(attended, i - 1)
                nc.scalar.activation(prob_t[i % 2][:, 0:4, 0:r], b6.rearrange("p (n t) -> p n t", n=4)[:, :, 0:r],
                                     ACT.Copy).then_inc(turn_a, 1)
                if i + 2 <= CH:
                    exps(i + 2)
                act.wait_ge(attended, i + 1)
                nc.scalar.activation(o_hi[:, :, P * i:P * i + r], ps_value[i % 2][:, :, 0:r],
                                     ACT.Copy).then_inc(o_hi_done, 1)
            for m in range(KD):
                if m % 2 == 0:
                    splits(Index(U_O + m // 2), 1)
                square_x(O_O, S_FFN, Index(m))
                nc.scalar.activation(a_hi[:, m, :], x_t[:, m, :], ACT.Copy,
                                     scale=vec[:, V_FFN + m:V_FFN + m + 1]).then_inc(act_hi, 1)
            split_hi(Index(U_FFN + 2))
            split_hi(Index(U_FFN + 3))

            def hidden(u0, j, c, first):
                if not (first and j == 0):
                    splits(u0 + 4 * j)
                if first and j == 0:
                    rms_root(S_FFN, rstd[:, :])
                act.wait_ge(g_conv, (c + 1).value())
                nc.scalar.activation(cv[0][:, 0:CEXT - 2], cv[0][:, 0:CEXT - 2], ACT.Silu).then_inc(g_silu, 1)
                splits(u0 + 4 * j + 2)
                act.wait_ge(h_prod, (c + 1).value())
                nc.scalar.activation(h_hi[:, j, 0:SEQ], cv[0][:, 0:SEQ], ACT.Copy).then_inc(h_hi_done, 1)
                nc.scalar.activation(by_smp(h_hi[:, j, SEQ:T]), smp(cv[0], 2)[:, :, 0:NT], ACT.Copy).then_inc(h_hi_done, 1)

            def group(u0, c0, first=False):
                for j in range(GRP):
                    hidden(u0, j, c0 + j, first)
                for m in range(KD):
                    splits(u0 + 4 * GRP + m, 1)

            group(Index(U_FFN), Index(0), first=True)
            with act.Fori(1, NG) as g:
                group(Index(U_FFN, g, FU), Index(0, g, GRP))
            for j in range(REST):
                hidden(Index(U_LAST), j, Index(NG * GRP + j), False)
            def final_root(n):
                act.wait_ge(ssq, S_FIN + n + 1)
                nc.scalar.activation(half(rstd, n), ps_b[:, n, 0:TH], ACT.Sqrt, bias=eps(), scale=1.0 / D).then_inc(root, 1)

            def final_square(i):
                n, m = divmod(i, KD)
                act.wait_ge(evacuated, O_LDN + i + 1)
                c = (S_FIN + n) * KD + m
                act.wait_ge(sq_added, c - 1)
                nc.scalar.activation(sq_tmp[:, c % 2, 0:TH], half(x_t[:, m, :], n), ACT.Square).then_inc(sq_done, 1)

            for i in range(KD):
                if i % 2 == 0:
                    splits(Index(U_LDN + i // 2), 1)
                if i >= 2:
                    final_square(i - 2)
            for i in range(KD - 2, 2 * KD):
                final_square(i)
                if i == KD + ROOT_AT:
                    final_root(0)
            final_root(1)

        @block.tensor
        def _(pe):
            def ident(n=P):
                return cst[0:n, C_ID:C_ID + n]

            def ones(n=P, m=P):
                return cst[0:n, C_ONE:C_ONE + m]

            def blocks(o, u, pairs, hi, lo, n, wait_chunk=None, late=False):
                s = u.mod(RING)
                pe.wait_ge(hi_ready, (u + 1).value())
                pe.wait_ge(lo_ready, (u + 1).value())
                for b, c, first, last, ends in pairs:
                    if wait_chunk is not None:
                        wait_chunk(c)
                    wh, wl = w_hi[:, s, P * b:P * b + P], w_lo[:, s, P * b:P * b + P]
                    terms = [(wh, hi), (wh, lo), (wl, hi)]
                    for t, (w, a) in enumerate(terms):
                        for k, m in enumerate(range(0, n[0] * n[1], n[1])):
                            ins_ = nc.tensor.matmul(out_bank(o, k)[:, 0:n[1]], w, a[:, c, m:m + n[1]],
                                                    start=first and t == 0, stop=last and t == 2)
                        if late and t == 0:
                            ins_.then_inc(half_used, 1)
                    if ends:
                        ins_.then_inc(half_used, 1)

            def free(o):
                if o.reg is not None or o.const >= 2:
                    pe.wait_ge(evacuated, (o - 1).value())

            def output(o, u, hi, lo, n=(2, TH), wait_chunk=None, between=None):
                free(o)
                for v in range(2):
                    if v and between is not None:
                        between()
                    pairs = [(b, UB * v + b, v == 0 and b == 0, v == 1 and b == UB - 1, b % 4 == 3)
                             for b in range(UB)]
                    blocks(o, u + v, pairs, hi, lo, n, wait_chunk)

            def chunk_waits(k0):
                def wait(c):
                    pe.wait_ge(act_hi, k0 + c + 1)
                    pe.wait_ge(act_lo, k0 + c + 1)
                return wait

            def sum_squares(group, n=T):
                pe.wait_ge(sq_added, (group + 1) * KD)
                for k in range(2):
                    m = nc.tensor.matmul(ps_b[:, k, 0:n // 2], ones(), sq_sum[:, k * n // 2:(k + 1) * n // 2],
                                         start=True, stop=True)
                m.then_inc(ssq, 1)

            def keep_warm(n):
                for _ in range(n):
                    nc.tensor.matmul(b4[:, 0:P], ident(), ones(), start=True, stop=True)

            pe.wait_ge(cst_in, 32)
            keep_warm(WARM_FIRST)
            for o in range(8):
                output(Index(O_MEM + o), Index(U_MEM + 2 * o), m_hi, m_lo, (1, NM),
                       chunk_waits(K_MEM) if o == 0 else None, (lambda: sum_squares(S_MEM, NM)) if o == 1 else None)
            output(Index(O_GATE), Index(U_GATE), a_hi, a_lo, wait_chunk=chunk_waits(K_MIX))
            pe.wait_ge(evacuated, O_MEM + 8)
            for h in range(H):
                for m in range(MT):
                    t = nc.tensor.transpose(ps_a[:, m, P * h:P * h + P], vt_mem[:, h, P * m:P * m + P], ident())
            t.then_inc(mv_tr, 1)
            pe.wait_ge(root, S_MEM + 1)
            sum_squares(S_MIX)

            def gates_by_token():
                pe.wait_ge(g_exps, 3)
                pe.wait_ge(mv_ready, MT)
                for q, row in enumerate((a_row, b_row)):
                    for c in range(CH + 1):
                        r = P if c < CH else NS
                        n = (q * (CH + 1) + c) * H
                        t = nc.tensor.transpose(b4[0:r, n:n + H], row[:, P * c:P * c + r], ident(H))
                t.then_inc(g_tr, 1)

            def head(h, i):
                def slot(j):
                    output(i.times(PAN) + (O_MIX + j), i.times(2 * PAN) + (U_MIX + 2 * j), a_hi, a_lo)

                slot(0)
                slot(1)
                slot(2)
                slot(3)
                pe.wait_ge(evacuated, (i.times(PAN) + O_MIX + 3).value())
                for c in range(CH):
                    nc.tensor.transpose(b4[:, P * c:P * c + P], qkv[:, 1, P * c:P * c + P], ident())
                    nc.tensor.transpose(b5[:, P * c:P * c + P], qkv[:, 2, P * c:P * c + P], ident())
                    nc.tensor.matmul(b7[:, P * c:P * c + P], qkv[:, 1, P * c:P * c + P], qkv[:, 0, P * c:P * c + P],
                                     start=True, stop=True)
                nc.tensor.transpose(b6[0:NS, 0:P], qkv[:, 1, SEQ:T], ident())
                nc.tensor.transpose(b6[0:NS, P:2 * P], qkv[:, 2, SEQ:T], ident())
                nc.tensor.matmul(b6[0:NS, 2 * P:2 * P + NS], qkv[:, 1, SEQ:T], qkv[:, 0, SEQ:T],
                                 start=True, stop=True).then_inc(tok_tr, 1)
                slot(4)
                pe.wait_ge(k_copied, (i + 1).times(CH + 1).value())
                pe.wait_ge(prods, (i + 1).value())
                pe.wait_ge(c_in, (i + 1).times(16).value())
                for c in range(CH):
                    nc.tensor.matmul(b4[:, P * c:P * c + P], k_tok[:, c, :], v_tok[:, c, :], start=True, stop=True)
                    nc.tensor.matmul(b7[:, c:c + 1], k_tok[:, c, :], ones(P, 1), start=True, stop=True)
                nc.tensor.matmul(b7[:, CH:CH + NB], k_tok[0:NS, CH, :], cst[0:NS, C_BLK:C_BLK + NB],
                                 start=True, stop=True)
                nc.tensor.matmul(b6, k_tok[0:NS, CH, :], vws[0][0:NS, :], start=True, stop=True)
                nc.tensor.matmul(b5[:, 64:64 + NS], ones(NS), dmat_s[:, :], start=True, stop=False)
                nc.tensor.matmul(b5[:, 64:64 + NS], ones(), nq[:, :], start=False, stop=True)
                for b in range(NB):
                    t0 = NT * b
                    nc.tensor.matmul(b5[:, t0:t0 + NT], c_smp[:, b, :], q_in[:, SEQ + t0:SEQ + t0 + NT],
                                     start=b == 0, stop=False, skip_group_check=True)
                nc.tensor.matmul(b5[:, 0:NS], v_tok[0:NS, CH, :], dmat_s[:, :], start=False, stop=True,
                                 skip_group_check=True).then_inc(updates, 1)
                slot(5)
                pe.wait_ge(chained, (i.times(2) + 1).value())
                for c in range(CH):
                    m = nc.tensor.matmul(b4[:, P * c:P * c + P], v_tok[:, c, :], dmat[:, c, :],
                                         start=True, stop=c == 0)
                    if c:
                        m = nc.tensor.matmul(b4[:, P * c:P * c + P], state[:, c - 1, 0:P], q_in[:, P * c:P * c + P],
                                             start=False, stop=True)
                nc.tensor.matmul(b7, ones(), den_t, start=True, stop=True)
                nc.tensor.matmul(b6, k_tok[0:NS, CH, :], vws[1][0:NS, :], start=True, stop=True).then_inc(sums, 1)
                slot(6)
                pe.wait_ge(h_sq, (i + 1).value())
                pe.wait_ge(chained, (i + 1).times(2).value())
                nc.tensor.matmul(b7, ones(), q_in[:, 0:SEQ], start=True, stop=True)
                nc.tensor.matmul(b6[:, 0:NS], ones(), q_in[:, SEQ:T], start=True, stop=True)
                pe.wait_ge(v_act, (i + 1).value())
                for c in range(CH):
                    nc.tensor.transpose(b4[:, P * c:P * c + P], va_t[:, P * c:P * c + P], ident())
                nc.tensor.transpose(b5[0:NS, 0:P], va_t[:, SEQ:T], ident()).then_inc(va_tr, 1)
                slot(7)
                pe.wait_ge(va_copied, (i + 1).times(2).value())
                pe.wait_ge(ws_ready, (i + 1).times(2).value())
                for c in range(CH):
                    nc.tensor.matmul(b4[:, P * c:P * c + P], va_tok[:, c, :], ws_t[:, :], start=True, stop=True)
                nc.tensor.matmul(b5[:, 0:NS], va_tok[0:NS, CH, :], wd_t[:, :], start=True, stop=True)
                pe.wait_ge(h_root, (i + 1).times(2).value())
                pe.wait_ge(pooled, (i + 1).value())
                pe.wait_ge(wp_in, (i + 1).times(16).value())
                nc.tensor.matmul(b6[:, 0:TH], wp_t[:, :], y_t[:, y_at("B", h), 0:TH], start=True, stop=True)
                nc.tensor.matmul(b7[:, 0:TH], wp_t[:, :], y_t[:, y_at("B", h), TH:T],
                                 start=True, stop=True).then_inc(mixed, 1)

            for j in range(2 * H):
                output(Index(O_PRE + j), Index(U_PRE + 2 * j), a_hi, a_lo)
                if j == 6:
                    gates_by_token()
            with pe.Fori(0, H) as h:
                head(h, Index(0, h, 1))
            output(Index(O_OUT), Index(U_OUT), a_hi, a_lo, wait_chunk=chunk_waits(K_Y))
            output(Index(O_OUT + 1), Index(U_OUT + 2), a_hi, a_lo)
            with pe.Fori(1, KD // 2) as m:
                for j in range(2):
                    output(Index(O_OUT + j, m, 2), Index(U_OUT + 2 * j, m, 4), a_hi, a_lo)
            output(Index(O_Q), Index(U_Q), a_hi, a_lo, wait_chunk=chunk_waits(K_CROSS))
            pe.wait_ge(a_done, H)
            pe.wait_ge(b_done, H)
            sum_squares(S_CROSS)
            for m in range(1, H):
                output(Index(O_Q + m), Index(U_Q + 2 * m), a_hi, a_lo)
            pe.wait_ge(evacuated, O_Q + H - 1)
            def scores(i):
                bank = ps_score[i % 2]
                if i >= 2:
                    pe.wait_ge(exped, H * (i - 1))
                if i < CH:
                    for h in range(H):
                        if i == 0 and h == H - 1:
                            pe.wait_ge(evacuated, O_Q + H)
                        m = nc.tensor.matmul(bank[:, h // 2, h % 2 * NM:(h % 2 + 1) * NM], q_t[:, h, P * i:P * i + P],
                                             mk_t[:, h, :], start=True, stop=True)
                else:
                    pe.wait_ge(pad_ready, 1)
                    pe.wait_ge(kc_in, 16)
                    for h in range(H):
                        for b in range(NB):
                            m = nc.tensor.matmul(bank[0:NS, h // 2, h % 2 * NM:(h % 2 + 1) * NM],
                                                 q_pad[h // 2][:, h % 2, b, :], kc_t[:, h, b, :],
                                                 start=b == 0, stop=b == NB - 1)
                m.then_inc(scored, 1)

            scores(0)
            scores(1)
            for i in range(CH + 1):
                r = P if i < CH else NS
                pe.wait_ge(normed, i + 1)
                for h in range(H):
                    for m in range(MT):
                        n = h * MT + m
                        t = nc.tensor.transpose(ps_b[:, n // 4, n % 4 * P:n % 4 * P + r],
                                                prob[i % 2][0:r, h, P * m:P * m + P], ident(r))
                t.then_inc(turned, 1)
                if i + 2 <= CH:
                    scores(i + 2)
                pe.wait_ge(turn_a, i + 1)
                pe.wait_ge(turn_v, i + 1)
                if i >= 2:
                    pe.wait_ge(o_lo_done, i - 1)
                value = ps_value[i % 2]
                if i < CH:
                    for h in range(H):
                        for m in range(MT):
                            v = nc.tensor.matmul(value[:, h, :], mv_t[:, m, P * h:P * h + P],
                                                 prob_t[i % 2][:, h * MT + m, :], start=m == 0, stop=m == MT - 1)
                else:
                    pe.wait_ge(vc_in, 16)
                    for h in range(H):
                        for b in range(NB):
                            for m in range(MT):
                                v = nc.tensor.matmul(value[:, h, NT * b:NT * b + NT], vc_t[:, b, m, P * h:P * h + P],
                                                     prob_t[i % 2][:, h * MT + m, NT * b:NT * b + NT],
                                                     start=m == 0, stop=m == MT - 1)
                v.then_inc(attended, 1)
            pe.wait_ge(o_hi_done, CH + 1)
            pe.wait_ge(o_lo_done, CH + 1)
            for m in range(KD):
                free(Index(O_O + m))
                a = 4 * (m % 2)
                blocks(Index(O_O + m), Index(U_O + m // 2), [(a + c, c, c == 0, c == H - 1, c == H - 1) for c in range(H)],
                       o_hi, o_lo, (2, TH))
            output(Index(O_FFN), Index(U_FFN), a_hi, a_lo, wait_chunk=chunk_waits(K_FFN))
            sum_squares(S_FFN)

            def hidden_waits(c0):
                def wait(c):
                    pe.wait_ge(h_hi_done, (c0 + c + 1).times(2).value())
                    pe.wait_ge(h_lo_done, (c0 + c + 1).times(2).value())
                return wait

            def down2(o, u, wait):
                for m in range(2):
                    free(o + m)
                    blocks(o + m, u + m, [(b, b, b == 0, False, m == 0 and b == 3) for b in range(GRP - 1)],
                           h_hi, h_lo, (2, TH), wait if m == 0 else None)
                for m in range(2):
                    blocks(o + m, u + m, [(GRP - 1, GRP - 1, False, True, True)], h_hi, h_lo, (2, TH),
                           wait if m == 0 else None, late=m == 1)

            def group(u0, o0, c0, first=0):
                for j in range(first, 2 * GRP):
                    output(o0 + j, u0 + 2 * j, a_hi, a_lo)
                down2(o0 + 2 * GRP, u0 + 4 * GRP, hidden_waits(c0))
                for m in range(2, KD):
                    free(o0 + 2 * GRP + m)
                    blocks(o0 + 2 * GRP + m, u0 + 4 * GRP + m,
                           [(b, b, b == 0, b == GRP - 1, b % 4 == 3) for b in range(GRP)], h_hi, h_lo, (2, TH))

            group(Index(U_FFN), Index(O_FFN), Index(0), first=1)
            with pe.Fori(1, NG) as g:
                group(Index(U_FFN, g, FU), Index(O_FFN, g, FO), Index(0, g, GRP))
            for j in range(2 * REST):
                output(Index(O_LAST + j), Index(U_LAST + 2 * j), a_hi, a_lo)
            def last_output(i, chunks):
                n, m = divmod(i, KD)
                u = Index(U_LDN + m // 2)
                if n == 0:
                    pe.wait_ge(hi_ready, (u + 1).value())
                    pe.wait_ge(lo_ready, (u + 1).value())
                w_h, w_l = split_place(u)
                for c in chunks:
                    b = REST * (m % 2) + c
                    if i == 0:
                        pe.wait_ge(h_hi_done, 2 * (NG * GRP + c + 1))
                        pe.wait_ge(h_lo_done, 2 * (NG * GRP + c + 1))
                    wh, wl = w_h[:, P * b:P * b + P], w_l[:, P * b:P * b + P]
                    for t, (w, a) in enumerate([(wh, h_hi), (wh, h_lo), (wl, h_hi)]):
                        mm = nc.tensor.matmul(last_bank(i), w, half(a[:, c, :], n), start=c == 0 and t == 0,
                                              stop=c == REST - 1 and t == 2)
                if REST - 1 in chunks:
                    mm.then_inc(half_used, 1)

            def final_sum(n):
                pe.wait_ge(sq_added, (S_FIN + n + 1) * KD)
                nc.tensor.matmul(ps_b[:, n, 0:TH], ones(), half(sq_sum, n), start=True, stop=True).then_inc(ssq, 1)

            keep_warm(WARM_LAST)
            for i in range(4):
                pe.wait_ge(evacuated, O_LDN - 1 + i // 2)
                last_output(i, range(REST - 1))
            for i in range(4):
                last_output(i, [REST - 1])
            for i in range(4, 2 * KD):
                pe.wait_ge(evacuated, O_LDN + i - 3)
                last_output(i, range(REST))
                if i == KD + ROOT_AT:
                    final_sum(0)
            final_sum(1)

        @block.vector
        def _(dve):
            tt, ts, stt = nc.vector.tensor_tensor, nc.vector.tensor_scalar, nc.vector.scalar_tensor_tensor
            copy = nc.vector.tensor_copy
            link = Chain(dve, dve_order)

            def splits(u, n=2):
                for k in range(2, n + 2):
                    if u.reg is None and u.const + k >= N_UNITS:
                        continue
                    s = (u + k).mod(RING)
                    dve.wait_ge(hi_ready, (u + k + 1).value())
                    hi, lo = split_place(u + k)
                    tt(lo, w_raw[:, s, :], hi, ALU.subtract).then_inc(lo_ready, 1)

            def chunk_lo(count, dst, src, hi, gain=None):
                dve.wait_ge(act_hi, count + 1)
                if gain is None:
                    tt(dst, src, hi, ALU.subtract).then_inc(act_lo, 1)
                else:
                    stt(dst, src, vec[:, gain:gain + 1], hi, ALU.mult, ALU.subtract).then_inc(act_lo, 1)

            def inv_root(group, r):
                dve.wait_ge(root, group + 1)
                nc.vector.reciprocal(r, r).then_inc(rstd_ready, 1)
                dve.wait_ge(rstd_ready, group + 1)

            def summed(u):
                dve.wait_ge(half_used, (u + 1).times(2).value())

            def evac(o, u, dst):
                summed(u)
                tt(halves(dst), out_view(o), halves(rstd[:, :]), ALU.mult).then_inc(evacuated, 1)

            def evac_ext(o, u, dst, before):
                summed(u)
                tt(dst[:, before:before + TH], out_bank(o, 0)[:, 0:TH], rstd[:, 0:TH], ALU.mult)
                tt(dst[:, before + TH:before + SEQ], out_bank(o, 1)[:, 0:SEQ - TH], rstd[:, TH:SEQ], ALU.mult)
                tt(smp(dst, before)[:, :, before:before + NT], by_smp(out_bank(o, 1)[:, SEQ - TH:TH]),
                   by_smp(rstd[:, SEQ:T]), ALU.mult).then_inc(evacuated, 1)
                dve.wait_ge(evacuated, (o + 1).value())

            def add_to_x(o, m):
                tt(halves(x_t[:, m, :]), out_view(o), halves(x_t[:, m, :]), ALU.add).then_inc(evacuated, 1)

            def conv3(dst, src, taps):
                n = CEXT - 2
                link(ts(dst[:, 0:n], src[:, 0:n], taps(0), None, ALU.mult))
                link(stt(dst[:, 0:n], src[:, 1:n + 1], taps(1), dst[:, 0:n], ALU.mult, ALU.add))
                return stt(dst[:, 0:n], src[:, 2:n + 2], taps(2), dst[:, 0:n], ALU.mult, ALU.add)

            splits(Index(-2), 1)
            dve.wait_ge(cst_in, 32)
            for k in range(KD):
                chunk_lo(K_MEM + k, m_lo[:, k, :], m_raw[:, k, :], m_hi[:, k, :], V_MEM + k)
                if k == 7:
                    splits(Index(-1), 1)
            splits(Index(0))
            dve.wait_ge(sq_done, KD)

            def mem_out(o):
                summed(Index(U_MEM + 2 * o + 1))
                dst = mk_t[:, o, :] if o < H else vt_mem[:, o - H, :]
                tt(dst, out_bank(Index(o), 0)[:, 0:NM], rstd_m, ALU.mult).then_inc(evacuated, 1)

            done = 0
            for o in range(8):
                u = U_MEM + 2 * o
                if o:
                    splits(Index(u))
                    for k in range(done, min(done + 3, KD) if o > 1 else 0):
                        chunk_lo(K_MIX + k, a_lo[:, k, :], x_t[:, k, :], a_hi[:, k, :], V_MIX + k)
                        done = k + 1
                if o == 1:
                    inv_root(S_MEM, rstd_m)
                    mem_out(0)
                if o:
                    mem_out(o)

            def scan(bufs, pad, shifts, op):
                a, b = bufs
                for s in shifts:
                    n = a.shape[2]
                    link(tt(b[:, :, pad:n], a[:, :, pad:n], a[:, :, pad - s:n - s], op))
                    a, b = b, a
                return a[:, :, pad:n]

            def by_chunk(row):
                return row.rearrange("p (c t) -> p c t", t=P)

            SHIFTS_P, SHIFTS_S = [1 << n for n in range(7)], [1, 2]

            def gates_1():
                dve.wait_ge(mv_ready, MT)
                for b in scan_p:
                    nc.vector.memset(b[:, :, 0:P // 2], 0.0)
                for b in scan_s:
                    nc.vector.memset(b[:, :, 0:2], 0.0)
                dve.wait_ge(evacuated, O_GATE + 1)
                link(ts(gate[:, :], gate[:, :], vec[:, V_BG:V_BG + 1], None, ALU.add))
                link(copy(b_row[:, :], gate[32:32 + H, :]))
                stt(f_row[:, :], b_row[:, :], -1.0, b_row[:, :], ALU.mult, ALU.min).then_inc(f_ready, 1)
                dve.wait_ge(f_exp, 1)
                ts(m_row[:, :], m_row[:, :], 1.0, None, ALU.add).then_inc(f_exp1, 1)

            def gates_2():
                dve.wait_ge(f_log, 1)
                lp, ls = scan_p[0][:, :, P // 2:], scan_s[0][:, :, 2:]
                stt(lp, by_chunk(b_row[:, 0:SEQ]), 0.0, by_chunk(w_row[:, 0:SEQ]), ALU.min, ALU.subtract)
                link(stt(ls, by_smp(b_row[:, SEQ:T]), 0.0, by_smp(w_row[:, SEQ:T]), ALU.min, ALU.subtract))
                bp = scan(scan_p, P // 2, SHIFTS_P, ALU.add)
                bs = scan(scan_s, 2, SHIFTS_S, ALU.add)
                copy(by_chunk(b_row[:, 0:SEQ]), bp)
                link(copy(by_smp(b_row[:, SEQ:T]), bs))
                link(tt(a_row[:, :], gate[0:H, :], b_row[:, :], ALU.subtract))

            def gates_3():
                for b in scan_p:
                    nc.vector.memset(b[:, :, 0:P // 2], -3.0e38)
                for b in scan_s:
                    nc.vector.memset(b[:, :, 0:2], -3.0e38)
                copy(scan_p[0][:, :, P // 2:], by_chunk(a_row[:, 0:SEQ]))
                link(copy(scan_s[0][:, :, 2:], by_smp(a_row[:, SEQ:T])))
                top_p = scan(scan_p, P // 2, SHIFTS_P, ALU.max)
                top_s = scan(scan_s, 2, SHIFTS_S, ALU.max)
                link(nc.vector.memset(m_prev[:, 0:1], 0.0))
                for c in range(CH):
                    t1 = P * c + P
                    link(ts(m_row[:, P * c:t1], top_p[:, c, :], m_prev[:, c:c + 1], None, ALU.max))
                    if c < CH - 1:
                        link(tt(m_prev[:, c + 1:c + 2], b_row[:, t1 - 1:t1], m_row[:, t1 - 1:t1], ALU.add))
                dve.wait_ge(smp_in, 16)
                link(tt(by_smp(m_row[:, SEQ:T]), top_s, ms_in[:, :].unsqueeze(2).broadcast_to([H, NB, NT]), ALU.max))

            def gates_4():
                m_p, m_s = by_chunk(m_row[:, 0:SEQ]), by_smp(m_row[:, SEQ:T])
                ts(r3[:, 0, :], m_row[:, :], -1.0, None, ALU.mult)
                tt(by_chunk(r3[:, 1, 0:SEQ]), m_p, m_prev[:, :].unsqueeze(2).broadcast_to([H, CH, P]), ALU.subtract)
                tt(by_smp(r3[:, 1, SEQ:T]), m_s, ms_in[:, :].unsqueeze(2).broadcast_to([H, NB, NT]), ALU.subtract)
                link(tt(w_row[:, :], b_row[:, :], m_row[:, :], ALU.add))
                tt(by_chunk(b_row[:, 0:SEQ]), by_chunk(a_row[:, 0:SEQ]), m_p[:, :, P - 1:P].broadcast_to([H, CH, P]),
                   ALU.subtract)
                tt(by_smp(b_row[:, SEQ:T]), by_smp(a_row[:, SEQ:T]), m_s[:, :, NT - 1:NT].broadcast_to([H, NB, NT]),
                   ALU.subtract).then_inc(g_rows, 1)

            splits(Index(U_GATE))
            inv_root(S_MIX, rstd[:, :])
            evac(Index(O_GATE), Index(U_GATE + 1), gate[:, :])
            steps = [gates_2, gates_3, gates_4]
            splits(Index(U_PRE))
            gates_1()
            for j in range(2 * H):
                if j:
                    splits(Index(U_PRE + 2 * j))
                evac(Index(O_PRE + j), Index(U_PRE + 2 * j + 1), y_t[:, y_at("C", j) if j < H else y_at("A", j - H), :])
                if j < len(steps):
                    steps[j]()
            dve.wait_ge(g_cols, 2)
            dve.wait_ge(rows_out, 32)
            dve.wait_ge(smp_in, 32)

            def mix_lo(k):
                chunk_lo(K_Y + k, a_lo[:, k, :], y_t[:, k, :], a_hi[:, k, :])

            def head(h, i, last=False):
                def o_(j):
                    return i.times(PAN) + (O_MIX + j)

                def u_(j):
                    return i.times(2 * PAN) + (U_MIX + 2 * j)

                def col(t, n):
                    return t[:, bass.ds(h + n, 1)]

                splits(u_(0))
                evac(o_(0), u_(0) + 1, qkv[:, 0, :])
                splits(u_(1))
                summed(u_(1) + 1)
                stt(halves(qkv[:, 1, :]), out_view(o_(1)), SCALE, halves(rstd[:, :]), ALU.mult, ALU.mult)\
                    .then_inc(evacuated, 1)
                splits(u_(2))
                evac(o_(2), u_(2) + 1, qkv[:, 2, :])
                dve.wait_ge(evacuated, (o_(2) + 1).value())
                dve.wait_ge(rows_in, (i + 1).times(16).value())
                link(tt(q_in[:, :], qkv[:, 0, :], rows[:, 1, :], ALU.mult))
                tt(by_smp(nq[:, :]), by_smp(q_in[:, SEQ:T]),
                   n_smp[:, h, :].unsqueeze(2).broadcast_to([P, NB, NT]), ALU.mult)
                for c in range(CH):
                    ts(dmat[:, c, :], rows[:, 0, P * c:P * c + P], cols[:, 0, c, bass.ds(h, 1)], 0.0, ALU.add, ALU.min)
                ts(dmat_s[:, :], rows[0:NS, 0, SEQ:T], cols[0:NS, 0, CH, bass.ds(h, 1)], 0.0, ALU.add, ALU.min)\
                    .then_inc(clamped, 1)
                splits(u_(3))
                evac(o_(3), u_(3) + 1, va_t[:, :])
                splits(u_(4))
                dve.wait_ge(tok_tr, (i + 1).value())
                copy(v_tok[:, 0:CH, :].rearrange("p c d -> p (c d)"), b5)
                dve.wait_ge(decayed, (i + 1).times(2).value())
                link(tt(dmat[:, :, :].rearrange("p c t -> p (c t)"), b7, dmat[:, :, :].rearrange("p c t -> p (c t)"),
                        ALU.mult))
                tt(dmat[:, :, :], dmat[:, :, :], cst[:, C_TRI:C_TRI + P].unsqueeze(1).broadcast_to([P, CH, P]), ALU.mult)
                dve.wait_ge(k_copied, (i + 1).times(CH + 1).value())
                copy(v_tok[0:NS, CH, :], b6[0:NS, P:2 * P])
                link(tt(dmat_s[:, :], b6[0:NS, 2 * P:2 * P + NS], dmat_s[:, :], ALU.mult))
                tt(dmat_s[:, :], dmat_s[:, :], cst[0:NS, C_STRI:C_STRI + NS], ALU.mult)
                for k in range(2):
                    blk = cst[0:NS, C_BLK + 4 * k:C_BLK + 4 * k + 4]
                    m = tt(vws[k][0:NS, :].rearrange("p (b d) -> p b d", d=P),
                           v_tok[0:NS, CH, :].unsqueeze(1).broadcast_to([NS, 4, P]),
                           blk.unsqueeze(2).broadcast_to([NS, 4, P]), ALU.mult)
                m.then_inc(prods, 1)
                link(nc.vector.memset(pe1[:, 0:PST], 0.0))
                evac_ext(o_(4), u_(4) + 1, pe1, PST)
                dve.wait_ge(ext_in, (i + 1).times(16).value())
                fac = [cst[:, bass.ds(h * 4 + (C_PF + k), 1)] for k in range(4)]
                y_b = y_t[:, y_at("B", h), :]
                t_p, t_s = qkv[:, 1, 0:PST + SEQ], rows[:, 0, 0:NB * (PST + NT)].rearrange("p (b t) -> p b t", b=NB)
                e_p, e_s = pe2[:, 0:PST + SEQ], smp(pe2, PST)
                link(stt(pe2[:, 1:PEXT], pe1[:, 0:PEXT - 1], fac[0], pe1[:, 1:PEXT], ALU.mult, ALU.add))
                stt(t_p[:, 3:], e_p[:, 1:PST + SEQ - 2], fac[1], e_p[:, 3:], ALU.mult, ALU.add)
                link(stt(t_s[:, :, 3:], e_s[:, :, 1:PST + NT - 2], fac[1], e_s[:, :, 3:], ALU.mult, ALU.add))
                stt(e_p[:, 7:], t_p[:, 3:PST + SEQ - 4], fac[2], t_p[:, 7:], ALU.mult, ALU.add)
                link(stt(e_s[:, :, 7:], t_s[:, :, 3:PST + NT - 4], fac[2], t_s[:, :, 7:], ALU.mult, ALU.add))
                stt(y_b[:, 0:SEQ], e_p[:, 7:PST + SEQ - 8], fac[3], e_p[:, PST:], ALU.mult, ALU.add)
                link(stt(by_smp(y_b[:, SEQ:T]), e_s[:, :, 7:PST + NT - 8], fac[3], e_s[:, :, PST:], ALU.mult, ALU.add))
                inv = cst[:, bass.ds(h * (PST + 1) + C_INV, PST)]
                link(tt(y_b[:, 0:PST], y_b[:, 0:PST], inv, ALU.mult))
                tt(y_b[:, 0:PST], y_b[:, 0:PST], pe1[:, PST:2 * PST], ALU.subtract)
                stt(y_b[:, PST:SEQ], y_b[:, PST:SEQ], col(cst, C_PW), pe1[:, 2 * PST:PST + SEQ], ALU.mult, ALU.subtract)
                stt(by_smp(y_b[:, SEQ:T]), by_smp(y_b[:, SEQ:T]), col(cst, C_PW), smp(pe1, PST)[:, :, PST:],
                    ALU.mult, ALU.subtract).then_inc(pooled, 1)
                splits(u_(5))
                dve.wait_ge(updates, (i + 1).value())
                copy(state[:, 0, 0:P], b4[:, 0:P])
                link(copy(state[:, 0, P:P + 1], b7[:, 0:1]))
                for c in range(1, CH):
                    dec = rows[:, 1, P * c + P - 1:P * c + P]
                    stt(state[:, c, 0:P], state[:, c - 1, 0:P], dec, b4[:, P * c:P * c + P], ALU.mult, ALU.add)
                    link(stt(state[:, c, P:P + 1], state[:, c - 1, P:P + 1], dec, b7[:, c:c + 1], ALU.mult, ALU.add))
                for b in range(NB // 2):
                    dec = rows[:, 1, SEQ + NT * b + NT - 1:SEQ + NT * b + NT]
                    stt(c_smp[:, b, :], c_smp[:, b, :], dec, b6[:, P * b:P * b + P], ALU.mult, ALU.add)
                n_new = n_smp[:, h, :]
                link(tt(n_new, n_new, by_smp(rows[:, 1, SEQ:T])[:, :, NT - 1], ALU.mult))
                tt(n_new, b7[:, CH:CH + NB], n_new, ALU.add)
                copy(den_t[:, 0:P], dmat[:, 0, :])
                for c in range(1, CH):
                    m = stt(den_t[:, P * c:P * c + P], q_in[:, P * c:P * c + P], state[:, c - 1, P:P + 1], dmat[:, c, :],
                            ALU.mult, ALU.add)
                m.then_inc(chained, 1)
                y_d = y_t[:, y_at("D", h), :]
                evac(o_(5), u_(5) + 1, y_d)
                splits(u_(6))
                dve.wait_ge(sums, (i + 1).value())
                stt(q_in[:, 0:SEQ], b7, -1.0, rows[:, 2, 0:SEQ], ALU.mult, ALU.max)
                link(stt(q_in[:, SEQ:T], b5[:, 64:64 + NS], -1.0, rows[:, 2, SEQ:T], ALU.mult, ALU.max))
                tt(q_in[:, 0:SEQ], b7, q_in[:, 0:SEQ], ALU.max)
                link(tt(q_in[:, SEQ:T], b5[:, 64:64 + NS], q_in[:, SEQ:T], ALU.max))
                link(nc.vector.reciprocal(q_in[:, :], q_in[:, :]))
                tt(h_t[:, 0:SEQ], b4, q_in[:, 0:SEQ], ALU.mult)
                tt(h_t[:, SEQ:T], b5[:, 0:NS], q_in[:, SEQ:T], ALU.mult).then_inc(h_ready, 1)
                for b in range(NB // 2, NB):
                    dec = rows[:, 1, SEQ + NT * b + NT - 1:SEQ + NT * b + NT]
                    m = stt(c_smp[:, b, :], c_smp[:, b, :], dec, b6[:, P * (b - 4):P * (b - 4) + P], ALU.mult, ALU.add)
                m.then_inc(chained, 1)
                dve.wait_ge(conv_in, (i + 1).times(16).value())
                link(nc.vector.memset(dx_e[:, 0:2], 0.0))
                evac_ext(o_(6), u_(6) + 1, dx_e, 2)
                tt(dx_e[:, 2:2 + SEQ], dx_e[:, 2:2 + SEQ], y_d[:, 0:SEQ], ALU.mult)
                link(tt(smp(dx_e, 2)[:, :, 2:], smp(dx_e, 2)[:, :, 2:], by_smp(y_d[:, SEQ:T]), ALU.mult))
                link(conv3(dcv, dx_e, lambda k: vec[:, bass.ds(h * 3 + (V_DC + k), 1)]))
                splits(u_(7))
                y_c = y_t[:, y_at("C", h), :]
                dve.wait_ge(h_root, (i + 1).times(2).value())
                link(nc.vector.reciprocal(q_in[:, :], q_in[:, :]))
                link(tt(h_t, h_t, q_in[:, :], ALU.mult))
                stt(y_c, h_t, col(vec, V_MN), y_c, ALU.mult, ALU.mult).then_inc(c_done, 1)
                if last:
                    dve.wait_ge(b_done, H - 1)
                    for k in range(y_at("C", h) + 1):
                        if k == y_at("C", h):
                            dve.wait_ge(c_done, H)
                        mix_lo(k)
                evac(o_(7), u_(7) + 1, y_d)
                dve.wait_ge(evacuated, (o_(7) + 1).value())
                tt(y_d[:, 0:SEQ], y_d[:, 0:SEQ], dcv[:, 0:SEQ], ALU.mult)
                tt(by_smp(y_d[:, SEQ:T]), by_smp(y_d[:, SEQ:T]), smp(dcv, 2)[:, :, 0:NT], ALU.mult).then_inc(d_done, 1)
                dve.wait_ge(mixed, (i + 1).value())
                dve.wait_ge(a_in, (i + 1).times(48).value())
                y_a = y_t[:, y_at("A", h), :]
                tt(va_t[:, 0:SEQ], b4, bs_t[:, 0:SEQ], ALU.add)
                link(tt(h_tmp[:, :], b5[:, 0:NS], bs_t[:, SEQ:T], ALU.add))
                tt(y_a[:, 0:SEQ], va_t[:, 0:SEQ], y_a[:, 0:SEQ], ALU.mult)
                tt(y_a[:, SEQ:T], h_tmp[:, :], y_a[:, SEQ:T], ALU.mult).then_inc(a_done, 1)
                if last:
                    dve.wait_ge(d_done, H)
                    mix_lo(y_at("D", h))
                ts(halves(y_b), ps_b[:, :, 0:TH], col(vec, V_PS), None, ALU.mult).then_inc(b_done, 1)
                if last:
                    dve.wait_ge(a_done, H)
                    mix_lo(y_at("A", h))

            dve.wait_ge(u_act, H)
            dve.wait_ge(o_gate, H)
            LINKS = 25
            with dve.Fori(0, H - 1) as h:
                link.enter(h, LINKS)
                head(h, Index(0, h, 1))
            link.leave(H - 1)
            head(H - 1, Index(H - 1), last=True)
            dve.wait_ge(b_done, H)
            mix_lo(y_at("B", H - 1))
            splits(Index(U_OUT))

            def out_proj(j, split=True):
                if split:
                    splits(j.times(2) + U_OUT)
                summed(j.times(2) + (U_OUT + 1))
                add_to_x(j + O_OUT, j.value())

            dve.wait_ge(x_back[0], 16)
            out_proj(Index(0), split=False)
            out_proj(Index(1))
            for n in range(1, 4):
                dve.wait_ge(x_back[n], 16)
            with dve.Fori(1, KD // 2 - 1) as m:
                for j in range(2):
                    out_proj(Index(j, m, 2))
            out_proj(Index(KD - 2))
            splits(Index(U_OUT + 2 * (KD - 1)))
            for k in range(12):
                chunk_lo(K_CROSS + k, a_lo[:, k, :], x_t[:, k, :], a_hi[:, k, :], V_CROSS + k)
            out_proj(Index(KD - 1), split=False)
            splits(Index(U_Q), 1)
            for k in range(12, KD):
                chunk_lo(K_CROSS + k, a_lo[:, k, :], x_t[:, k, :], a_hi[:, k, :], V_CROSS + k)
            splits(Index(U_Q + 1), 1)
            inv_root(S_CROSS, rstd[:, :])
            for m in range(H):
                if m:
                    splits(Index(U_Q + 2 * m))
                evac(Index(O_Q + m), Index(U_Q + 2 * m + 1), q_t[:, m, :])
            def tops(i):
                r = P if i < CH else NS
                dve.wait_ge(scored, i + 1)
                scores = ps_score[i % 2][0:r, :, :].rearrange("p a (h m) -> p (a h) m", m=NM)
                link(nc.vector.tensor_reduce(top[i % 2][0:r, :], scores, AX.X, ALU.max))
                ts(neg_top[i % 2][0:r, :], top[i % 2][0:r, :], -SCALE, None, ALU.mult).then_inc(topped, 1)

            def over_sum(i):
                r = P if i < CH else NS
                dve.wait_ge(exped, H * (i + 1))
                link(nc.vector.reciprocal(p_inv[i % 2][0:r, :], p_sum[i % 2][0:r, :]))
                tt(prob[i % 2][0:r, :, :], prob[i % 2][0:r, :, :],
                   p_inv[i % 2][0:r, :].unsqueeze(2).broadcast_to([r, H, NM]), ALU.mult).then_inc(normed, 1)

            dve.wait_ge(evacuated, O_Q + H)
            tops(0)
            tops(1)
            over_sum(0)
            dve.wait_ge(pad_zero, 2)
            for b in range(NB):
                for k in range(2):
                    m = copy(q_pad[k][:, :, b, NT * b:NT * b + NT], q_t[:, 2 * k:2 * k + 2, SEQ + NT * b:SEQ + NT * b + NT])
            m.then_inc(pad_ready, 1)
            for i in range(CH + 1):
                r = P if i < CH else NS
                dve.wait_ge(turned, i + 1)
                if i >= 2:
                    dve.wait_ge(attended, i - 1)
                copy(prob_t[i % 2][:, 4:8, 0:r], b7.rearrange("p (n t) -> p n t", n=4)[:, :, 0:r]).then_inc(turn_v, 1)
                if i + 1 <= CH:
                    over_sum(i + 1)
                if i + 2 <= CH:
                    tops(i + 2)
                dve.wait_ge(o_hi_done, i + 1)
                tt(o_lo[:, :, P * i:P * i + r], ps_value[i % 2][:, :, 0:r], o_hi[:, :, P * i:P * i + r], ALU.subtract)\
                    .then_inc(o_lo_done, 1)
            def ffn_lo(k):
                chunk_lo(K_FFN + k, a_lo[:, k, :], x_t[:, k, :], a_hi[:, k, :], V_FFN + k)

            for m in range(KD):
                if m % 2 == 0:
                    splits(Index(U_O + m // 2), 1)
                dve.wait_ge(half_used, 2 * U_O + m + 1)
                add_to_x(Index(O_O + m), m)
                if 0 < m <= FREE_LO:
                    ffn_lo(m - 1)
            for k in range(FREE_LO, KD):
                ffn_lo(k)
            splits(Index(U_FFN))
            inv_root(S_FFN, rstd[:, :])
            dve.wait_ge(fs_in, 32)
            for e in ext:
                link(nc.vector.memset(e[:, 0:2], 0.0))

            def hidden(u0, o0, j, c, first):
                for k in range(2):
                    n = (c.times(2) + k).value()
                    if not (first and j == 0 and k == 0):
                        splits(u0 + (4 * j + 2 * k))
                    old = f_state[:, n, 0:2 * NB].rearrange("p (b t) -> p b t", t=2)
                    ts(smp(ext[k], 2)[:, :, 0:2], old, 1.0, None, ALU.mult)
                    evac_ext(o0 + (2 * j + k), u0 + (4 * j + 2 * k + 1), ext[k], 2)
                    m = conv3(cv[k], ext[k], lambda t: f_taps[:, n, t:t + 1])
                    if k == 0:
                        m.then_inc(g_conv, 1)
                    else:
                        link(m)
                    ts(old, smp(ext[k], 2)[:, :, NT:NT + 2], 1.0, None, ALU.mult)
                    link(ts(f_state[:, n, 2 * NB:2 * NB + 2], ext[k][:, SEQ:SEQ + 2], 1.0, None, ALU.mult))
                dve.wait_ge(g_silu, (c + 1).value())
                tt(cv[0][:, 0:CEXT - 2], cv[0][:, 0:CEXT - 2], cv[1][:, 0:CEXT - 2], ALU.mult).then_inc(h_prod, 1)
                dve.wait_ge(h_hi_done, (c + 1).times(2).value())
                tt(h_lo[:, j, 0:SEQ], cv[0][:, 0:SEQ], h_hi[:, j, 0:SEQ], ALU.subtract).then_inc(h_lo_done, 1)
                tt(by_smp(h_lo[:, j, SEQ:T]), smp(cv[0], 2)[:, :, 0:NT], by_smp(h_hi[:, j, SEQ:T]), ALU.subtract)\
                    .then_inc(h_lo_done, 1)

            def group(u0, o0, c0, first=False):
                for j in range(GRP):
                    hidden(u0, o0, j, c0 + j, first)
                for m in range(KD):
                    splits(u0 + (4 * GRP + m), 1)
                    summed(u0 + (4 * GRP + m))
                    add_to_x(o0 + (2 * GRP + m), m)

            group(Index(U_FFN), Index(O_FFN), Index(0), first=True)
            with dve.Fori(1, NG) as g:
                link.enter(g, GRP * 7, 1)
                group(Index(U_FFN, g, FU), Index(O_FFN, g, FO), Index(0, g, GRP))
            link.leave(NG - 1, 1)
            for j in range(REST):
                hidden(Index(U_LAST), Index(O_LAST), j, Index(NG * GRP + j), False)
            def final_scale(n):
                dve.wait_ge(root, S_FIN + n + 1)
                nc.vector.reciprocal(half(rstd, n), half(rstd, n)).then_inc(rstd_ready, 1)
                dve.wait_ge(rstd_ready, S_FIN + n + 1)

            def final_norm(n, k):
                y = half(x_t[:, k, :], n)
                stt(y, y, vec[:, V_FIN + k:V_FIN + k + 1], half(rstd, n), ALU.mult, ALU.mult).then_inc(y_done, 1)

            normed_y = 0
            for i in range(2 * KD):
                n, m = divmod(i, KD)
                if n == 0 and m % 2 == 0:
                    splits(Index(U_LDN + m // 2), 1)
                dve.wait_ge(half_used, 2 * U_LDN + i + 1)
                x = half(x_t[:, m, :], n)
                tt(x, last_bank(i), x, ALU.add).then_inc(evacuated, 1)
                if i == KD + NORM_AT - 1:
                    final_scale(0)
                if n and m >= NORM_AT:
                    for k in range(2 if m < 2 * NORM_AT else 1):
                        final_norm(0, normed_y)
                        normed_y += 1
            final_scale(1)
            for k in range(KD):
                final_norm(1, k)


def weight_units(i):
    def cols(w, a):
        return w[:, a:a + P]

    def panel(w):
        k = w.shape[0] // P
        return w.reshape(k // UB, UB, P, P).transpose(0, 2, 1, 3).reshape(k // UB, P, UB * P)

    w_in, w_up, w_down, w_o = i["w_in"][0], i["w_up"][0], i["w_down"][0], i["w_o"][0]
    out = np.zeros((N_UNITS, P, UB * P), np.float32)
    at = 0

    def put(units):
        nonlocal at
        out[at:at + units.shape[0], :, 0:units.shape[2]] = units
        at += units.shape[0]

    for n in range(8):
        put(panel(cols(i["w_kv"][0], P * n)))
    gates = np.zeros((D, P), np.float32)
    gates[:, 0:H] = w_in[:, 10 * GW:10 * GW + H]
    gates[:, 32:32 + H] = w_in[:, 10 * GW + H:10 * GW + 2 * H]
    put(panel(gates))
    for part in (6, 0):
        for h in range(H):
            put(panel(cols(w_in, part * GW + P * h)))
    for h in range(H):
        for part in (3, 4, 5, 1, 2, 8, 9, 7):
            put(panel(cols(w_in, part * GW + P * h)))
    w_out = i["w_out"][0].reshape(4, H, P, D)[["ABCD".index(x) for x in MIXERS]].swapaxes(0, 1).reshape(D, D)
    for m in range(KD):
        put(panel(cols(w_out, P * m)))
    for m in range(H):
        put(panel(cols(i["w_q"][0], P * m)))
    for m in range(0, KD, 2):
        put(panel(np.concatenate([cols(w_o, P * m), cols(w_o, P * m + P)])))
    for c0 in range(0, JF, GRP):
        n = min(GRP, JF - c0)
        for c in range(c0, c0 + n):
            put(panel(cols(w_up, P * c)))
            put(panel(cols(w_up, DFF + P * c)))
        rows = w_down[P * c0:P * (c0 + n)]
        if n == GRP:
            for m in range(KD):
                put(panel(cols(rows, P * m)))
        else:
            for m in range(0, KD, 2):
                two = np.concatenate([cols(rows, P * m), cols(rows, P * m + P)])
                put(two.reshape(1, 2 * n, P, P).transpose(0, 2, 1, 3).reshape(1, P, 2 * n * P))
    assert at == N_UNITS
    return out


def constants():
    c = np.zeros((P, N_CST), np.float32)
    c[:, C_ID:C_ID + P] = np.eye(P)
    c[:, C_ONE:C_ONE + P] = 1
    c[:, C_TRI:C_TRI + P] = np.triu(np.ones((P, P)))
    for b in range(NB):
        s = slice(NT * b, NT * b + NT)
        c[s, C_STRI + NT * b:C_STRI + NT * b + NT] = np.triu(np.ones((NT, NT)))
        c[s, C_BLK + b] = 1
    for h in range(H):
        w = 2 ** (h + 1)
        for k in range(4):
            c[:, C_PF + 4 * h + k] = float(k <= h)
        c[:, C_PW + h] = 1.0 / w
        for t in range(PST + 1):
            c[:, C_INV + (PST + 1) * h + t] = 1.0 / min(t + 1, w)
    c[:, C_EPS] = EPS
    return c


def by_feature(v):
    v = v.reshape(v.shape[:-1] + (v.shape[-1] // P, P))
    return np.ascontiguousarray(np.moveaxis(np.moveaxis(v, -1, 0), -1, 1))


def vectors(i):
    v = np.zeros((P, N_VEC), np.float32)
    for at, name in ((V_MEM, "mem_norm"), (V_MIX, "norm_mix"), (V_CROSS, "norm_cross"), (V_FFN, "norm_ffn")):
        v[:, at:at + KD] = by_feature(i[name][0])
    v[:, V_FIN:V_FIN + KD] = by_feature(i["final_norm"])
    v[0:H, V_BG] = i["b_gate"][0, 0:H]
    v[32:32 + H, V_BG] = i["b_gate"][0, H:2 * H]
    v[:, V_PS:V_PS + H] = by_feature(i["pool_scale"][0])
    v[:, V_MN:V_MN + H] = by_feature(i["mlstm_norm"][0])
    v[:, V_DC:V_DC + 3 * H] = by_feature(i["w_dconv"][0]).reshape(P, 3 * H)
    return v


def laid_out(i):
    f = np.float32
    x = np.concatenate([i["x_prompt"][0], i["x_sample"].reshape(NS, D)])
    w_s, b_s = i["w_s"][0], i["b_s"][0]
    w_s_smp = np.zeros((H, NS, NS), f)
    for b in range(NB):
        s = slice(NT * b, NT * b + NT)
        w_s_smp[:, s, s] = w_s[:, 0:NT, 0:NT].transpose(0, 2, 1)
    kc = i["cache_mem_k"][0].transpose(3, 2, 0, 1)
    vc = i["cache_mem_v"][0].reshape(NB, MT, P, GW).transpose(2, 0, 1, 3)
    up = i["state_ffn_conv"][0]
    pair = by_feature(up).reshape(P, 2, JF, NB, 2).transpose(0, 2, 1, 3, 4).reshape(P, 2 * JF, 2 * NB)
    taps = by_feature(i["w_fconv"][0]).reshape(P, 2, JF, 3).transpose(0, 2, 1, 3).reshape(P, 2 * JF, 3)
    heads = lambda a: a.reshape(NB, -1, H, P).transpose(2, 3, 0, 1)
    return {
        "wall": weight_units(i),
        "x": by_feature(x),
        "mem": by_feature(i["mem_prompt"][0]),
        "cst": constants(),
        "vec": vectors(i),
        "m_smp": i["state_mlstm_m"][0].T,
        "n_smp": i["state_mlstm_n"][0].transpose(2, 1, 0),
        "c_smp": i["state_mlstm_c"][0].transpose(1, 3, 0, 2),
        "b_s": np.concatenate([np.tile(b_s, (1, CH)), np.tile(b_s[:, 0:NT], (1, NB))], axis=1),
        "w_s": w_s.transpose(0, 2, 1),
        "w_s_smp": w_s_smp,
        "w_pool": i["w_pool"][0],
        "pool_st": heads(i["state_pool"][0]),
        "conv_st": heads(i["state_conv"][0]),
        "k_cache": kc,
        "v_cache": vc,
        "ffn_st": pair,
        "w_fconv": taps,
    }


OUTPUTS = {
    "y": (P, KD, T), "mem_k": (P, H, NM), "mem_v": (P, MT, GW), "m_all": (H, T),
    "c_p": (H, P, P + 1), "c_s": (H, P, NB, P), "n_s": (H, P, NB), "v_rows": (H, P, NS),
    "pool_p": (H, P, PST), "pool_s": (H, P, NB, PST), "conv_p": (H, P, 2), "conv_s": (H, P, NB, 2),
    "ffn_st": (P, 2 * JF, 2 * NB + 2),
}


def kernel(**inputs):
    import concourse.bacc as bacc
    from concourse.bass_utils import run_bass_kernel_spmd

    i = {k: np.asarray(v) for k, v in inputs.items()}
    arrays, ins, outs = {}, {}, {}
    nc = bacc.Bacc("TRN2", target_bir_lowering=False, num_devices=1)
    for name, a in laid_out(i).items():
        arrays["in_" + name] = a = np.ascontiguousarray(a)
        ins[name] = nc.dram_tensor("in_" + name, a.shape, mybir.dt.from_np(a.dtype), kind="ExternalInput").ap()
    for name, shape in OUTPUTS.items():
        outs[name] = nc.dram_tensor("out_" + name, shape, F32, kind="ExternalOutput").ap()
    build(nc, ins, outs)
    r = run_bass_kernel_spmd(nc, [arrays], core_ids=[0]).results[0]
    o = {name: np.asarray(r["out_" + name]) for name in OUTPUTS}

    y = o["y"].transpose(2, 1, 0).reshape(T, D)
    per_head = lambda a: a.transpose(*range(2, a.ndim), 0, 1).reshape(a.shape[2:] + (GW,))
    ffn = o["ffn_st"].reshape(P, JF, 2, 2 * NB + 2).transpose(3, 2, 1, 0).reshape(2 * NB + 2, 2 * DFF)
    c_p, m_all = o["c_p"], o["m_all"]
    out = (
        y[None, 0:SEQ], y[SEQ:].reshape(NB, NT, D),
        per_head(o["pool_p"])[None, None], per_head(o["conv_p"])[None, None],
        c_p[:, :, 0:P].transpose(0, 2, 1)[None, None], c_p[:, :, P][None, None], m_all[:, SEQ - 1][None, None],
        ffn[2 * NB:][None, None],
        o["mem_k"].transpose(2, 1, 0)[None, None], o["mem_v"].transpose(1, 0, 2).reshape(NM, H, P)[None, None],
        per_head(o["v_rows"]).reshape(1, NB, NT, GW), per_head(o["pool_s"])[None], per_head(o["conv_s"])[None],
        o["c_s"].transpose(2, 0, 3, 1)[None], o["n_s"].transpose(2, 0, 1)[None],
        m_all[:, SEQ:].reshape(H, NB, NT)[:, :, NT - 1].T[None], ffn[0:2 * NB].reshape(1, NB, 2, 2 * DFF),
    )
    return tuple(np.ascontiguousarray(a) for a in out)
```
